# Optimizing a Trainium2 kernel written in Bass

```python
import jax, jax.numpy as jnp
from jax import lax
import numpy as np
import math

D_MODEL = 1024
BATCH = 1
SEQ = 512
DEPTH = 2

A_GROUPS = 8
A_GROUP_DIM = 64
A_WIDTH = A_GROUPS * A_GROUP_DIM
A_CHUNK = 128
B_HEADS = 8
B_HEAD_DIM = 64
B_WIDTH = B_HEADS * B_HEAD_DIM
B_BRANCHES = ((128, 1), (512, 4), (2048, 16))
B_BLOCK = 128
C_HEADS = 4
C_DK = 128
C_DV = 256
C_GATE_RANK = 16
C_TAU = 16.0
C_CHUNK = 64
D_FF = 2816
CONV_W = 3

EPS = 1e-6
NEG = -1e30
N_EVEN = (DEPTH + 1) // 2
N_ODD = DEPTH // 2
EVEN_IN = 2 * A_WIDTH + 3 * B_WIDTH
ODD_IN = 2 * C_HEADS * C_DK + 2 * C_HEADS * C_DV + C_GATE_RANK


def rms_norm(x, g):
    xf = x.astype(jnp.float32)
    return xf * lax.rsqrt(jnp.mean(xf * xf, -1, keepdims=True) + EPS) * g.astype(jnp.float32)

def layer_norm(x, g, b):
    xf = x.astype(jnp.float32)
    mu = jnp.mean(xf, -1, keepdims=True)
    xc = xf - mu
    return xc * lax.rsqrt(jnp.mean(xc * xc, -1, keepdims=True) + EPS) * g + b

def causal_dwconv(h, w, b):
    S = h.shape[1]
    hp = jnp.pad(h, ((0, 0), (CONV_W - 1, 0), (0, 0)))
    out = b
    for k in range(CONV_W):
        out = out + hp[:, k:k + S] * w[k]
    return out

def chunked_gmlp(u, v, ln_g, ln_b, w_s, b_s):
    Bn, S, _ = u.shape
    nc = S // A_CHUNK
    vn = layer_norm(v, ln_g, ln_b).reshape(Bn, nc, A_CHUNK, A_GROUPS, A_GROUP_DIM)
    causal = jnp.tril(jnp.ones((A_CHUNK, A_CHUNK), dtype=bool))
    ws = jnp.where(causal[None], w_s.astype(jnp.float32), 0.0)
    mixed = jnp.einsum('gts,bnsgc->bntgc', ws, vn) + b_s.astype(jnp.float32).T[:, :, None]
    return u.astype(jnp.float32) * mixed.reshape(Bn, S, A_WIDTH)

def dilated_branch(q, k, v, window, dilation):
    Bn, H, S, hd = q.shape
    span = dilation * B_BLOCK
    Sp = -(-S // span) * span
    M = Sp // dilation
    nb = M // B_BLOCK
    n_back = window // dilation

    def to_blocks(t):
        t = jnp.pad(t, ((0, 0), (0, 0), (0, Sp - S), (0, 0)))
        t = t.reshape(Bn, H, M, dilation, hd)
        t = jnp.moveaxis(t, 3, 2)
        return t.reshape(Bn, H, dilation, nb, B_BLOCK, hd)

    def band(t):
        tp = jnp.pad(t, ((0, 0), (0, 0), (0, 0), (1, 0), (0, 0), (0, 0)))
        return jnp.concatenate([tp[:, :, :, :-1], tp[:, :, :, 1:]], axis=4)

    qb = to_blocks(q)
    kk = band(to_blocks(k))
    vv = band(to_blocks(v))

    i = jnp.arange(B_BLOCK)[:, None]
    j = jnp.arange(2 * B_BLOCK)[None, :]
    dist = B_BLOCK + i - j
    in_band = (dist >= 0) & (dist <= n_back)
    valid = in_band[None] & ((jnp.arange(nb) > 0)[:, None, None] | (j >= B_BLOCK)[None])

    s = jnp.einsum('bhrnic,bhrnjc->bhrnij', qb, kk) * (hd ** -0.5)
    s = jnp.where(valid, s, NEG)
    m = jnp.max(s, -1, keepdims=True)
    p = jnp.exp(s - m)
    den = jnp.sum(p, -1)
    o = jnp.einsum('bhrnij,bhrnjc->bhrnic', p, vv) / den[..., None]
    lse = m[..., 0] + jnp.log(den)

    def from_blocks(t):
        tail = t.shape[5:]
        t = t.reshape((Bn, H, dilation, M) + tail)
        t = jnp.moveaxis(t, 2, 3).reshape((Bn, H, Sp) + tail)
        return t[:, :, :S]

    return from_blocks(o), from_blocks(lse)

def even_mixer(h, w_in, a_ln_g, a_ln_b, a_ws, a_bs, q_g, k_g, w_out):
    Bn, S, _ = h.shape
    z = h @ w_in
    u, v, q, k, vb = jnp.split(
        z, [A_WIDTH, 2 * A_WIDTH, 2 * A_WIDTH + B_WIDTH, 2 * A_WIDTH + 2 * B_WIDTH], axis=-1)
    a_out = chunked_gmlp(jax.nn.gelu(u, approximate=False), jax.nn.gelu(v, approximate=False),
                         a_ln_g, a_ln_b, a_ws, a_bs)

    def heads(t):
        return t.reshape(Bn, S, B_HEADS, B_HEAD_DIM).transpose(0, 2, 1, 3)

    qh = rms_norm(heads(q), q_g)
    kh = rms_norm(heads(k), k_g)
    vh = heads(vb).astype(jnp.float32)
    outs, lses = [], []
    for window, dilation in B_BRANCHES:
        o_r, l_r = dilated_branch(qh, kh, vh, window, dilation)
        outs.append(o_r)
        lses.append(l_r)
    wts = jax.nn.softmax(jnp.stack(lses), axis=0)
    o = jnp.einsum('rbhs,rbhsc->bhsc', wts, jnp.stack(outs))
    b_out = o.transpose(0, 2, 1, 3).reshape(Bn, S, B_WIDTH)
    return jnp.concatenate([a_out, b_out], axis=-1).astype(h.dtype) @ w_out

def gla_chunked(q, k, v, log_a):
    Bn, H, S, dk = q.shape
    dv = v.shape[-1]
    nc = S // C_CHUNK

    def rs(t):
        return t.reshape(Bn, H, nc, C_CHUNK, t.shape[-1])

    q, k, v, log_a = rs(q), rs(k), rs(v), rs(log_a)
    b = jnp.cumsum(log_a, axis=3)
    b_last = b[:, :, :, -1:]
    q_t = q * jnp.exp(b)
    k_t = k * jnp.exp(-b)
    k_s = k * jnp.exp(b_last - b)
    causal = jnp.tril(jnp.ones((C_CHUNK, C_CHUNK), dtype=bool))
    attn = jnp.where(causal, jnp.einsum('bhnik,bhnjk->bhnij', q_t, k_t), 0.0)
    o_intra = jnp.einsum('bhnij,bhnjv->bhniv', attn, v)
    kv = jnp.einsum('bhnjk,bhnjv->bhnkv', k_s, v)
    decay = jnp.exp(b_last[:, :, :, 0])

    def step(state, inp):
        kv_n, d_n = inp
        return d_n[..., None] * state + kv_n, state

    init = jnp.zeros((Bn, H, dk, dv), jnp.float32)
    _, states = lax.scan(step, init, (jnp.moveaxis(kv, 2, 0), jnp.moveaxis(decay, 2, 0)))
    states = jnp.moveaxis(states, 0, 2)
    o_inter = jnp.einsum('bhnik,bhnkv->bhniv', q_t, states)
    return (o_intra + o_inter).reshape(Bn, H, S, dv)

def gla_mixer(h, w_in, w_a2, b_a, head_g, w_out):
    Bn, S, _ = h.shape
    hk, hv = C_HEADS * C_DK, C_HEADS * C_DV
    z = h @ w_in
    q, k, v, r, ga = jnp.split(z, [hk, 2 * hk, 2 * hk + hv, 2 * hk + 2 * hv], axis=-1)

    def heads(t, dh):
        return t.reshape(Bn, S, C_HEADS, dh).transpose(0, 2, 1, 3).astype(jnp.float32)

    log_a = jax.nn.log_sigmoid((ga @ w_a2 + b_a).astype(jnp.float32)) / C_TAU
    o = gla_chunked(heads(q, C_DK) * (C_DK ** -0.5), heads(k, C_DK), heads(v, C_DV),
                    heads(log_a, C_DK))
    o = rms_norm(o, head_g)
    o = o.transpose(0, 2, 1, 3).reshape(Bn, S, hv) * jax.nn.silu(r.astype(jnp.float32))
    return o.astype(h.dtype) @ w_out

def conv_ffn(h, w_gate, w_up, conv_w, conv_b, w_down):
    g = causal_dwconv(h @ w_gate, conv_w, conv_b)
    return (jax.nn.silu(g) * (h @ w_up)) @ w_down

def first_inputs(seed: int = 0) -> dict:
    key = jax.random.key(seed)
    ks = iter(jax.random.split(key, 32))

    def nrm(shape, scale):
        return jax.random.normal(next(ks), shape, jnp.float32) * scale

    res = (2 * DEPTH) ** -0.5
    return {
        "x": nrm((BATCH, SEQ, D_MODEL), 1.0),
        "norm_mix_g": 1.0 + nrm((DEPTH, D_MODEL), 0.1),
        "norm_ffn_g": 1.0 + nrm((DEPTH, D_MODEL), 0.1),
        "ev_w_in": nrm((N_EVEN, D_MODEL, EVEN_IN), D_MODEL ** -0.5),
        "ev_a_ln_g": 1.0 + nrm((N_EVEN, A_WIDTH), 0.1),
        "ev_a_ln_b": nrm((N_EVEN, A_WIDTH), 0.02),
        "ev_a_ws": nrm((N_EVEN, A_GROUPS, A_CHUNK, A_CHUNK), A_CHUNK ** -0.5),
        "ev_a_bs": 1.0 + nrm((N_EVEN, A_GROUPS, A_CHUNK), 0.1),
        "ev_q_g": 1.0 + nrm((N_EVEN, B_HEAD_DIM), 0.1),
        "ev_k_g": 1.0 + nrm((N_EVEN, B_HEAD_DIM), 0.1),
        "ev_w_out": nrm((N_EVEN, A_WIDTH + B_WIDTH, D_MODEL), (A_WIDTH + B_WIDTH) ** -0.5 * res),
        "od_w_in": nrm((N_ODD, D_MODEL, ODD_IN), D_MODEL ** -0.5),
        "od_w_a2": nrm((N_ODD, C_GATE_RANK, C_HEADS * C_DK), C_GATE_RANK ** -0.5),
        "od_b_a": nrm((N_ODD, C_HEADS * C_DK), 0.5),
        "od_head_g": 1.0 + nrm((N_ODD, C_DV), 0.1),
        "od_w_out": nrm((N_ODD, C_HEADS * C_DV, D_MODEL), (C_HEADS * C_DV) ** -0.5 * res),
        "ffn_w_gate": nrm((DEPTH, D_MODEL, D_FF), D_MODEL ** -0.5),
        "ffn_w_up": nrm((DEPTH, D_MODEL, D_FF), D_MODEL ** -0.5),
        "ffn_conv_w": nrm((DEPTH, CONV_W, D_FF), CONV_W ** -0.5),
        "ffn_conv_b": nrm((DEPTH, D_FF), 0.02),
        "ffn_w_down": nrm((DEPTH, D_FF, D_MODEL), D_FF ** -0.5 * res),
    }

def first_block(x, norm_mix_g, norm_ffn_g,
              ev_w_in, ev_a_ln_g, ev_a_ln_b, ev_a_ws, ev_a_bs, ev_q_g, ev_k_g, ev_w_out,
              od_w_in, od_w_a2, od_b_a, od_head_g, od_w_out,
              ffn_w_gate, ffn_w_up, ffn_conv_w, ffn_conv_b, ffn_w_down):
    for layer in range(DEPTH):
        h = rms_norm(x, norm_mix_g[layer]).astype(x.dtype)
        if layer % 2 == 0:
            e = layer // 2
            mix = even_mixer(h, ev_w_in[e], ev_a_ln_g[e], ev_a_ln_b[e], ev_a_ws[e], ev_a_bs[e],
                             ev_q_g[e], ev_k_g[e], ev_w_out[e])
        else:
            o = layer // 2
            mix = gla_mixer(h, od_w_in[o], od_w_a2[o], od_b_a[o], od_head_g[o], od_w_out[o])
        x = x + mix.astype(x.dtype)
        h = rms_norm(x, norm_ffn_g[layer]).astype(x.dtype)
        x = x + conv_ffn(h, ffn_w_gate[layer], ffn_w_up[layer], ffn_conv_w[layer],
                         ffn_conv_b[layer], ffn_w_down[layer]).astype(x.dtype)
    return x


N_HEADS_ATTN = 8
HEAD_DIM = 64
N_KV_GROUPS = 2
HEADS_PER_GROUP = N_HEADS_ATTN // N_KV_GROUPS
D_ATTN = N_HEADS_ATTN * HEAD_DIM
D_KV = N_KV_GROUPS * HEAD_DIM
D_CONV = D_MODEL - D_ATTN
CONV_WIDTH = 3
CMP_BLOCK = 32
CMP_STRIDE = 16
CMP_OVERLAP = CMP_BLOCK // CMP_STRIDE
CMP_HIDDEN = 256
SEL_BLOCK = 64
SEL_RATIO = SEL_BLOCK // CMP_STRIDE
N_SELECT = 16
WINDOW = 512
Q_BLOCK = 128
ROPE_THETA = 500000.0
ROPE_DIM = HEAD_DIM // 4
N_GATES = 3 * N_HEADS_ATTN
D_IN_PROJ = D_ATTN + 6 * D_KV + N_GATES + 3 * D_CONV
NEG_INF = -1e30
FORCE_SCORE = 1e9
MAX_POS_OFFSET = 1024
SCALE = 1.0 / math.sqrt(HEAD_DIM)


def rms_norm_2(x, g):
    xf = x.astype(jnp.float32)
    y = xf * lax.rsqrt(jnp.mean(xf * xf, axis=-1, keepdims=True) + EPS)
    return (y * g.astype(jnp.float32)).astype(x.dtype)

def swiglu(x, w_gate, w_up, w_down):
    return (jax.nn.silu(x @ w_gate) * (x @ w_up)) @ w_down

def partial_rope(x, positions):
    half = ROPE_DIM // 2
    inv_freq = ROPE_THETA ** (-jnp.arange(half, dtype=jnp.float32) * 2.0 / ROPE_DIM)
    ang = positions.astype(jnp.float32)[..., None] * inv_freq
    cos = jnp.cos(ang)[:, :, None, :]
    sin = jnp.sin(ang)[:, :, None, :]
    xf = x.astype(jnp.float32)
    x1, x2, rest = xf[..., :half], xf[..., half:ROPE_DIM], xf[..., ROPE_DIM:]
    out = jnp.concatenate([x1 * cos - x2 * sin, x2 * cos + x1 * sin, rest], axis=-1)
    return out.astype(x.dtype)

def compress_blocks(k, pe, w1, w2):
    B, S, G, dk = k.shape
    n_chunks = S // CMP_STRIDE
    n_cmp = n_chunks - CMP_OVERLAP + 1
    chunks = k.reshape(B, n_chunks, CMP_STRIDE, G, dk)
    blocks = jnp.concatenate([chunks[:, j:j + n_cmp] for j in range(CMP_OVERLAP)], axis=2)
    blocks = blocks + pe[None, None, :, None, :]
    flat = blocks.transpose(0, 1, 3, 2, 4).reshape(B, n_cmp, G, CMP_BLOCK * dk)
    return jax.nn.gelu(flat @ w1) @ w2

def nsa_group(q, k_cmp, v_cmp, k_slc, v_slc, k_win, v_win, gates, positions,
              pe_k, w1_k, w2_k, pe_v, w1_v, w2_v):
    B, S = q.shape[:2]
    H, G, HPG, dk = N_HEADS_ATTN, N_KV_GROUPS, HEADS_PER_GROUP, HEAD_DIM
    q_raw = q.reshape(B, S, H, dk)
    q_rot = partial_rope(q_raw, positions)
    k_slc = partial_rope(k_slc.reshape(B, S, G, dk), positions)
    v_slc = v_slc.reshape(B, S, G, dk)
    k_win = partial_rope(k_win.reshape(B, S, G, dk), positions)
    v_win = v_win.reshape(B, S, G, dk)
    kc = compress_blocks(k_cmp.reshape(B, S, G, dk), pe_k, w1_k, w2_k)
    vc = compress_blocks(v_cmp.reshape(B, S, G, dk), pe_v, w1_v, w2_v)
    n_cmp = kc.shape[1]
    cmp_end = jnp.arange(n_cmp) * CMP_STRIDE + CMP_BLOCK - 1
    n_sel = S // SEL_BLOCK
    k_top = min(N_SELECT, n_sel)
    kb = k_slc.reshape(B, n_sel, SEL_BLOCK, G, dk).transpose(0, 3, 1, 2, 4)
    vb = v_slc.reshape(B, n_sel, SEL_BLOCK, G, dk).transpose(0, 3, 1, 2, 4)
    kw = jnp.pad(k_win, ((0, 0), (WINDOW, 0), (0, 0), (0, 0)))
    vw = jnp.pad(v_win, ((0, 0), (WINDOW, 0), (0, 0), (0, 0)))
    g = jax.nn.sigmoid(gates.astype(jnp.float32)).reshape(B, S, H, 3)
    agg_w = [float(c) for c in np.convolve(np.ones(SEL_RATIO), np.ones(CMP_OVERLAP))]
    pad_front = CMP_OVERLAP - 1
    pad_back = SEL_RATIO * n_sel + len(agg_w) - 1 - SEL_RATIO - n_cmp - pad_front + 1
    b_idx = jnp.arange(B)[:, None, None, None]
    g_idx = jnp.arange(G)[None, :, None, None]
    blk_j = jnp.arange(n_sel)

    def one_block(qb):
        s0 = qb * Q_BLOCK
        t = s0 + jnp.arange(Q_BLOCK)
        qr = lax.dynamic_slice_in_dim(q_raw, s0, Q_BLOCK, axis=1).reshape(B, Q_BLOCK, G, HPG, dk)
        qs = lax.dynamic_slice_in_dim(q_rot, s0, Q_BLOCK, axis=1).reshape(B, Q_BLOCK, G, HPG, dk)
        gb = lax.dynamic_slice_in_dim(g, s0, Q_BLOCK, axis=1)
        sc = jnp.einsum('bqghd,bngd->bghqn', qr, kc).astype(jnp.float32) * SCALE
        valid_c = cmp_end[None, :] <= t[:, None]
        pc = jax.nn.softmax(jnp.where(valid_c, sc, NEG_INF), axis=-1) * valid_c.astype(jnp.float32)
        o_cmp = jnp.einsum('bghqn,bngd->bqghd', pc.astype(vc.dtype), vc)
        imp = jnp.pad(pc.sum(axis=2), ((0, 0), (0, 0), (0, 0), (pad_front, pad_back)))
        p_slc = agg_w[0] * imp[..., 0:SEL_RATIO * n_sel:SEL_RATIO]
        for o in range(1, len(agg_w)):
            p_slc = p_slc + agg_w[o] * imp[..., o:o + SEL_RATIO * n_sel:SEL_RATIO]
        cur = (t // SEL_BLOCK)[:, None]
        valid_b = blk_j[None, :] * SEL_BLOCK <= t[:, None]
        forced = (blk_j[None, :] == 0) | (blk_j[None, :] == cur) | (blk_j[None, :] == cur - 1)
        score = jnp.where(valid_b, jnp.where(forced, FORCE_SCORE, p_slc), NEG_INF)
        _, idx = lax.top_k(score, k_top)
        kg = kb[b_idx, g_idx, idx].reshape(B, G, Q_BLOCK, k_top * SEL_BLOCK, dk)
        vg = vb[b_idx, g_idx, idx].reshape(B, G, Q_BLOCK, k_top * SEL_BLOCK, dk)
        tok = idx[..., None] * SEL_BLOCK + jnp.arange(SEL_BLOCK)
        mask_s = (tok <= t[None, None, :, None, None]).reshape(B, G, Q_BLOCK, k_top * SEL_BLOCK)
        ss = jnp.einsum('bqghd,bgqkd->bghqk', qs, kg).astype(jnp.float32) * SCALE
        ps = jax.nn.softmax(jnp.where(mask_s[:, :, None], ss, NEG_INF), axis=-1)
        o_slc = jnp.einsum('bghqk,bgqkd->bqghd', ps.astype(vg.dtype), vg)
        kwb = lax.dynamic_slice_in_dim(kw, s0, WINDOW + Q_BLOCK, axis=1)
        vwb = lax.dynamic_slice_in_dim(vw, s0, WINDOW + Q_BLOCK, axis=1)
        kpos = s0 - WINDOW + jnp.arange(WINDOW + Q_BLOCK)
        diff = t[:, None] - kpos[None, :]
        mask_w = (diff >= 0) & (diff < WINDOW) & (kpos[None, :] >= 0)
        sw = jnp.einsum('bqghd,bkgd->bghqk', qs, kwb).astype(jnp.float32) * SCALE
        pw = jax.nn.softmax(jnp.where(mask_w, sw, NEG_INF), axis=-1)
        o_win = jnp.einsum('bghqk,bkgd->bqghd', pw.astype(vwb.dtype), vwb)
        o = (gb[..., 0:1] * o_cmp.reshape(B, Q_BLOCK, H, dk).astype(jnp.float32)
             + gb[..., 1:2] * o_slc.reshape(B, Q_BLOCK, H, dk).astype(jnp.float32)
             + gb[..., 2:3] * o_win.reshape(B, Q_BLOCK, H, dk).astype(jnp.float32))
        return o.astype(q.dtype).reshape(B, Q_BLOCK, H * dk)

    out = lax.map(one_block, jnp.arange(S // Q_BLOCK))
    return out.transpose(1, 0, 2, 3).reshape(B, S, D_ATTN)

def short_conv_group(bg, cg, xc, w_conv):
    u = cg * xc
    y = lax.conv_general_dilated(u, w_conv[:, None, :].astype(u.dtype), window_strides=(1,),
                                 padding=[(CONV_WIDTH - 1, 0)],
                                 dimension_numbers=('NWC', 'WIO', 'NWC'),
                                 feature_group_count=D_CONV)
    return bg * y

def hybrid_mixer(h, positions, w_in, pe_k, w1_k, w2_k, pe_v, w1_v, w2_v,
                 w_conv, attn_out_norm, conv_out_norm, w_out):
    z = h @ w_in
    sizes = [D_ATTN] + [D_KV] * 6 + [N_GATES] + [D_CONV] * 3
    cuts = [int(c) for c in np.cumsum(sizes)[:-1]]
    q, kc, vc, ks, vs, kw, vw, gates, bg, cg, xc = jnp.split(z, cuts, axis=-1)
    attn = nsa_group(q, kc, vc, ks, vs, kw, vw, gates, positions, pe_k, w1_k, w2_k, pe_v, w1_v, w2_v)
    conv = short_conv_group(bg, cg, xc, w_conv)
    merged = jnp.concatenate([rms_norm_2(attn, attn_out_norm), rms_norm_2(conv, conv_out_norm)], axis=-1)
    return merged @ w_out

def second_inputs(seed: int = 0) -> dict:
    key = jax.random.key(seed)
    ks = jax.random.split(key, 26)
    L = DEPTH

    def nrm(k, shape, scale):
        return jax.random.normal(k, shape, jnp.float32) * scale

    def gain(k, n):
        return 1.0 + 0.05 * jax.random.normal(k, (L, n), jnp.float32)

    x = nrm(ks[0], (BATCH, SEQ, D_MODEL), 1.0)
    positions = (jnp.arange(SEQ, dtype=jnp.int32)[None, :]
                 + jax.random.randint(ks[1], (BATCH, 1), 0, MAX_POS_OFFSET, dtype=jnp.int32))
    return {
        "x": x,
        "positions": positions,
        "ffn1_norm_pre": gain(ks[2], D_MODEL),
        "ffn1_w_gate": nrm(ks[3], (L, D_MODEL, D_FF), D_MODEL ** -0.5),
        "ffn1_w_up": nrm(ks[4], (L, D_MODEL, D_FF), D_MODEL ** -0.5),
        "ffn1_w_down": nrm(ks[5], (L, D_FF, D_MODEL), D_FF ** -0.5),
        "ffn1_norm_post": gain(ks[6], D_MODEL),
        "mix_norm_pre": gain(ks[7], D_MODEL),
        "w_in": nrm(ks[8], (L, D_MODEL, D_IN_PROJ), D_MODEL ** -0.5),
        "cmp_pe_k": nrm(ks[9], (L, CMP_BLOCK, HEAD_DIM), 0.02),
        "cmp_w1_k": nrm(ks[10], (L, CMP_BLOCK * HEAD_DIM, CMP_HIDDEN), (CMP_BLOCK * HEAD_DIM) ** -0.5),
        "cmp_w2_k": nrm(ks[11], (L, CMP_HIDDEN, HEAD_DIM), CMP_HIDDEN ** -0.5),
        "cmp_pe_v": nrm(ks[12], (L, CMP_BLOCK, HEAD_DIM), 0.02),
        "cmp_w1_v": nrm(ks[13], (L, CMP_BLOCK * HEAD_DIM, CMP_HIDDEN), (CMP_BLOCK * HEAD_DIM) ** -0.5),
        "cmp_w2_v": nrm(ks[14], (L, CMP_HIDDEN, HEAD_DIM), CMP_HIDDEN ** -0.5),
        "conv_w": nrm(ks[15], (L, CONV_WIDTH, D_CONV), CONV_WIDTH ** -0.5),
        "attn_out_norm": gain(ks[16], D_ATTN),
        "conv_out_norm": gain(ks[17], D_CONV),
        "w_out": nrm(ks[18], (L, D_MODEL, D_MODEL), D_MODEL ** -0.5),
        "mix_norm_post": gain(ks[19], D_MODEL),
        "ffn2_norm_pre": gain(ks[20], D_MODEL),
        "ffn2_w_gate": nrm(ks[21], (L, D_MODEL, D_FF), D_MODEL ** -0.5),
        "ffn2_w_up": nrm(ks[22], (L, D_MODEL, D_FF), D_MODEL ** -0.5),
        "ffn2_w_down": nrm(ks[23], (L, D_FF, D_MODEL), D_FF ** -0.5),
        "ffn2_norm_post": gain(ks[24], D_MODEL),
    }

def second_block(x, positions, ffn1_norm_pre, ffn1_w_gate, ffn1_w_up, ffn1_w_down, ffn1_norm_post,
              mix_norm_pre, w_in, cmp_pe_k, cmp_w1_k, cmp_w2_k, cmp_pe_v, cmp_w1_v, cmp_w2_v,
              conv_w, attn_out_norm, conv_out_norm, w_out, mix_norm_post,
              ffn2_norm_pre, ffn2_w_gate, ffn2_w_up, ffn2_w_down, ffn2_norm_post):
    for l in range(DEPTH):
        h = swiglu(rms_norm_2(x, ffn1_norm_pre[l]), ffn1_w_gate[l], ffn1_w_up[l], ffn1_w_down[l])
        x = x + 0.5 * rms_norm_2(h, ffn1_norm_post[l])
        h = hybrid_mixer(rms_norm_2(x, mix_norm_pre[l]), positions, w_in[l],
                         cmp_pe_k[l], cmp_w1_k[l], cmp_w2_k[l], cmp_pe_v[l], cmp_w1_v[l], cmp_w2_v[l],
                         conv_w[l], attn_out_norm[l], conv_out_norm[l], w_out[l])
        x = x + rms_norm_2(h, mix_norm_post[l])
        h = swiglu(rms_norm_2(x, ffn2_norm_pre[l]), ffn2_w_gate[l], ffn2_w_up[l], ffn2_w_down[l])
        x = x + 0.5 * rms_norm_2(h, ffn2_norm_post[l])
    return x


def setup_inputs(seed=0):
    out = dict(first_inputs(seed))
    for name, value in second_inputs(seed + 1).items():
        if name != "x":
            out[name + "_2"] = value
    return out


def reference(
    x, norm_mix_g, norm_ffn_g, ev_w_in, ev_a_ln_g, ev_a_ln_b, ev_a_ws, ev_a_bs, ev_q_g, ev_k_g,
    ev_w_out, od_w_in, od_w_a2, od_b_a, od_head_g, od_w_out, ffn_w_gate, ffn_w_up, ffn_conv_w,
    ffn_conv_b, ffn_w_down, positions_2, ffn1_norm_pre_2, ffn1_w_gate_2, ffn1_w_up_2,
    ffn1_w_down_2, ffn1_norm_post_2, mix_norm_pre_2, w_in_2, cmp_pe_k_2, cmp_w1_k_2, cmp_w2_k_2,
    cmp_pe_v_2, cmp_w1_v_2, cmp_w2_v_2, conv_w_2, attn_out_norm_2, conv_out_norm_2, w_out_2,
    mix_norm_post_2, ffn2_norm_pre_2, ffn2_w_gate_2, ffn2_w_up_2, ffn2_w_down_2,
    ffn2_norm_post_2,
):
    x = first_block(
        x, norm_mix_g, norm_ffn_g, ev_w_in, ev_a_ln_g, ev_a_ln_b, ev_a_ws, ev_a_bs, ev_q_g,
        ev_k_g, ev_w_out, od_w_in, od_w_a2, od_b_a, od_head_g, od_w_out, ffn_w_gate, ffn_w_up,
        ffn_conv_w, ffn_conv_b, ffn_w_down,
    )
    return second_block(
        x, positions_2, ffn1_norm_pre_2, ffn1_w_gate_2, ffn1_w_up_2, ffn1_w_down_2,
        ffn1_norm_post_2, mix_norm_pre_2, w_in_2, cmp_pe_k_2, cmp_w1_k_2, cmp_w2_k_2,
        cmp_pe_v_2, cmp_w1_v_2, cmp_w2_v_2, conv_w_2, attn_out_norm_2, conv_out_norm_2, w_out_2,
        mix_norm_post_2, ffn2_norm_pre_2, ffn2_w_gate_2, ffn2_w_up_2, ffn2_w_down_2,
        ffn2_norm_post_2,
    )


_drawn_inputs = setup_inputs


def setup_inputs(seed=0):
    import zlib

    import numpy as np

    out = dict(_drawn_inputs(seed))
    spreads = {}
    factors = {'ev_a_ln_b': 8.0,
     'ev_q_g': 5.195,
     'ev_k_g': 4.489,
     'ffn_conv_b': 4.357,
     'cmp_pe_k_2': 8.0,
     'cmp_pe_v_2': 2.941,
     'ffn2_norm_post_2': 2.714}
    for name, (base, spread) in spreads.items():
        noise = np.random.default_rng([zlib.crc32(name.encode()), seed]).standard_normal(out[name].shape)
        drawn = base * np.exp(spread * noise) if base else spread * noise
        out[name] = __import__('jax').numpy.asarray(drawn.astype(out[name].dtype))
    for name, factor in factors.items():
        out[name] = (out[name] * factor).astype(out[name].dtype)
    return out
```

```python
from contextlib import ExitStack

import numpy as np

import concourse.bass as bass
from concourse import mybir

F32 = mybir.dt.float32
F32R = mybir.dt.float32r
I32 = mybir.dt.int32
ALU = mybir.AluOpType
ACT = mybir.ActivationFunctionType
AX = mybir.AxisListType

P = 128
T = 512
D = 1024
KT = D // P
FF = 2816
FT = FF // P
FPAIRS = FT // 2
EPS = 1e-6
NEG = -1e30
CW = 256
HD = 64
CHUNK = KT * CW
TT = T // P

N_NORMS = 10
N_POST = 6
PC = {}


def _columns():
    at = 0
    for name, n in (("norm", N_NORMS * 8), ("post", N_POST * 8), ("lng", 4), ("lnb", 4), ("qkg", 2),
                    ("fcw", 2 * FT * 3), ("fcb", 2 * FT), ("ba", 4), ("hg", 2), ("cw", 2 * 12),
                    ("aon", 8), ("con", 8), ("pe", 64), ("freq", 1), ("rotm", 1), ("restm", 1)):
        PC[name] = at
        at += n
    return at


PCOLS = _columns()

DOWN_K = (8, 8, 6)
EVEN_IN = 10
ODD_IN = 13
B_IN = 16
OUT = 4
FFN_IN = 2 * FPAIRS
FFN_DOWN = 12
N_CHUNKS = EVEN_IN + OUT + ODD_IN + OUT + 2 * (B_IN + OUT) + 6 * (FFN_IN + FFN_DOWN)


class Count:

    def __init__(self):
        self.n, self.per, self.i = {}, {}, None
        self.chunk = self.group = 0

    def __call__(self, sem, k=1):
        self.n[id(sem)] = self.n.get(id(sem), 0) + k
        v, per = self.n[id(sem)], self.per.get(id(sem), 0)
        return v + self.i * per if per else v

    def skip(self, sem, k=1):
        self.n[id(sem)] = self.n.get(id(sem), 0) + k

    def loop(self, eng, trips, body):
        before, marks = dict(self.n), (self.chunk, self.group)
        body(Nowhere(), 0)
        per = {k: v - before.get(k, 0) for k, v in self.n.items() if v != before.get(k, 0)}
        moved = (self.chunk - marks[0], self.group - marks[1])
        self.n, (self.chunk, self.group) = dict(before), marks
        with eng.Fori(0, trips, 1) as i:
            self.per, self.i = per, i
            body(eng, i)
        self.per, self.i = {}, None
        self.n = {**before, **{k: before.get(k, 0) + trips * v for k, v in per.items()}}
        self.chunk, self.group = marks[0] + trips * moved[0], marks[1] + trips * moved[1]


class Nowhere:

    def _self(self, *a, **k):
        return self

    wait_ge = then_inc = activation = tensor_tensor = tensor_scalar = scalar_tensor_tensor = _self
    tensor_copy = reciprocal = memset = matmul = transpose = dma_start = copy_predicated = _self
    tensor_tensor_scan = tensor_tensor_reduce = _self


def two(t, m):
    return t[:, bass.ds(2 * m, 2), :]


def tile(t, m):
    return t[:, bass.ds(m, 1), :].rearrange("p o n -> p (o n)")


def over_tiles(row, n=2):
    return row.unsqueeze(1).to_broadcast([row.shape[0], n, row.shape[1]])


class Core:

    def __init__(self, nc, ctx):
        self.nc = nc

        def at(name, shape, offset, dt=F32, parts=P):
            t = nc.alloc_sbuf_tensor_at(name, [parts, *shape], dt, offset=offset)
            n = -(-int(np.prod(shape)) * 4 // 32) * 32
            return t, offset + n

        base = -(-nc.sbuf_base // 32) * 32
        self.x, o = at("x", [KT, T], base)
        HH = o
        self.h_hi, o = at("h_hi", [KT, T], HH, F32R)
        HL = o
        self.h_lo, o = at("h_lo", [KT, T], HL, F32R)
        MH = o
        self.hid_hi, o = at("hid_hi", [FT, T], MH, F32R)
        ML = o
        self.hid_lo, o = at("hid_lo", [FT, T], ML, F32R)
        self.stage, o = at("stage", [2, CHUNK], o)
        self.w_hi, o = at("w_hi", [2, KT, CW], o, F32R)
        self.w_lo, o = at("w_lo", [2, KT, CW], o, F32R)
        self.rstd, o = at("rstd", [T], o)
        self.acc, o = at("acc", [2, T], o)
        SC = o
        self.sq, o = at("sq", [2, T], SC)
        VA = o
        self.val, o = at("val", [2, T], VA)
        self.gate, o = at("gate", [2, T + 2], o)
        self.par, o = at("par", [PCOLS], o)
        self.ident, o = at("ident", [P], o)
        self.ones, o = at("ones", [P], o)
        self.blockones, o = at("blockones", [P], o)
        self.stat, o = at("stat", [64], o)
        self.eps = self.stat[:, 60:61]
        self.one = self.ones[:, 0:1]
        assert o <= base + 212800, o
        self.y, _ = at("y", [KT, T], HH)
        M1, M2 = MH + 8 * T * 4, ML + 8 * T * 4
        self.ev_qk, _ = at("ev_qk", [8, T], M1)
        self.ev_u, _ = at("ev_u", [4, T], M1 + 16384)
        self.ev_mask, _ = at("ev_mask", [T], M1 + 24576)
        self.tri, _ = at("tri", [P], M1 + 26624)
        self.ev_v, _ = at("ev_v", [4, T], M2)
        self.ev_vb, _ = at("ev_vb", [4, T], M2 + 8192)
        self.ev_vtok, _ = at("ev_vtok", [TT, 512], M2 + 16384)
        self.ev_ws, _ = at("ev_ws", [8, P], M2 + 24576)
        self.ev_vntok, _ = at("ev_vntok", [TT, 512], HH)
        self.ev_bs, _ = at("ev_bs", [4, P], HH + 8192)
        self.qs, _ = at("qs", [T], HH + 10240)
        self.ks, _ = at("ks", [T], HH + 12288)
        self.vs, _ = at("vs", [TT, P], HH + 14336)
        self.score, _ = at("score", [3, T], HL)
        self.probT, _ = at("probT", [2, T], HL + 6144)
        self.gp, _ = at("gp", [24], HL + 10240)
        self.qs2, _ = at("qs2", [T], HL + 10368)
        self.od_q, _ = at("od_q", [4, T], M1)
        self.od_k, _ = at("od_k", [4, T], M1 + 8192)
        self.od_b, _ = at("od_b", [T], M1 + 16384)
        self.od_e1, _ = at("od_e1", [T], M1 + 18432)
        self.od_e2, _ = at("od_e2", [T], M1 + 20480)
        self.od_e3, _ = at("od_e3", [T], M1 + 22528)
        self.od_qt, _ = at("od_qt", [T], M1 + 24576)
        self.od_kt, _ = at("od_kt", [T], M1 + 26624)
        self.od_vtok, _ = at("od_vtok", [TT, 1024], M2)
        self.od_kstok, _ = at("od_kstok", [TT, P], M2 + 16384)
        self.od_at, _ = at("od_at", [TT, P], M2 + 18432)
        self.od_ga, _ = at("od_ga", [T], M2 + 20480)
        self.od_reset, _ = at("od_reset", [T], M2 + 22528)
        self.od_wa, _ = at("od_wa", [512], M2 + 24576)
        self.od_mask, _ = at("od_mask", [P], M2 + 26624, I32)
        self.od_was, _ = at("od_was", [P], M2 + 27136)
        self.od_decays, _ = at("od_decays", [4, 8], M2 + 27648)
        self.od_decay, _ = at("od_decay", [8], M2 + 27776)
        self.od_kstoks, _ = at("od_kstoks", [4, T], ML + 8192)
        self.od_vs, _ = at("od_vs", [TT, CW], HH)
        self.od_state, _ = at("od_state", [8, CW], HH + 4096)
        self.od_t1, _ = at("od_t1", [T], ML)
        self.od_t2, _ = at("od_t2", [T], ML + 2048)
        self.od_std, _ = at("od_std", [T], HH + 12288)
        self.od_r, _ = at("od_r", [8, T], MH)
        self.b_q, _ = at("b_q", [4, T], M1)
        self.b_qr, _ = at("b_qr", [4, T], M1 + 8192)
        self.b_u, _ = at("b_u", [4, T], M1 + 16384)
        self.b_ks, _ = at("b_ks", [2, T], M1 + 24576)
        self.b_r, _ = at("b_r", [2, 2, T], M2)
        self.b_a_hi, _ = at("b_a_hi", [2, 16 * 64], M2 + 8192, F32R)
        self.b_a_lo, _ = at("b_a_lo", [2, 16 * 64], M2 + 16384, F32R)
        self.b_vs, _ = at("b_vs", [2, TT, P], M2 + 24576)
        self.b_kw, _ = at("b_kw", [2, T], MH)
        self.b_g, _ = at("b_g", [TT, 24], MH + 4096)
        self.b_cos, _ = at("b_cos", [T], MH + 4480)
        self.b_sin, _ = at("b_sin", [T], MH + 6528)
        self.b_ang, _ = at("b_ang", [T], MH + 8576)
        self.b_pos, _ = at("b_pos", [T], MH + 10624, I32)
        self.b_sel, _ = at("b_sel", [5, P], MH + 12672)
        self.b_cmask, _ = at("b_cmask", [TT, 32], MH + 15232)
        self.b_valid, _ = at("b_valid", [1], MH + 15744)
        self.b_y, _ = at("b_y", [4, T], ML)
        self.b_mask, _ = at("b_mask", [T], ML + 8192)
        self.b_w2k, _ = at("b_w2k", [2, P], ML + 10240)
        self.b_w2v, _ = at("b_w2v", [2, HD], ML + 11264)
        self.b_kc, _ = at("b_kc", [64], ML + 11776)
        self.b_vc, _ = at("b_vc", [2, HD], ML + 12032)
        self.b_h, _ = at("b_h", [CW], ML + 12544)
        self.b_hT, _ = at("b_hT", [2, 64], ML + 13568)

        self.ps = [nc.alloc_psum_tensor(f"main{i}", [P, 2, T], F32) for i in range(2)]
        self.m = [nc.alloc_psum_tensor(f"misc{i}", [P, T], F32) for i in range(4)]
        def sem(name):
            return ctx.enter_context(nc.semaphore(name))

        self.params_loaded = sem("params_loaded")
        self.x_loaded = sem("x_loaded")
        self.ident_loaded = sem("ident_loaded")
        self.ones_loaded = sem("ones_loaded")
        self.blockones_loaded = sem("blockones_loaded")
        self.stored = sem("stored")
        self.last_ready = sem("last_ready")
        self.eps_ready = sem("eps_ready")
        self.post_y = sem("post_y")
        self.w_hi_done = sem("w_hi_done")
        self.w_lo_done = sem("w_lo_done")
        self.chunk_done = sem("chunk_done")
        self.group_taken = sem("group_taken")
        self.h_hi_done = sem("h_hi_done")
        self.h_lo_done = sem("h_lo_done")
        self.x_ready = sem("x_ready")
        self.sq_ready = sem("sq_ready")
        self.acc_ready = sem("acc_ready")
        self.ssq_ready = sem("ssq_ready")
        self.std_ready = sem("std_ready")
        self.rstd_ready = sem("rstd_ready")
        self.const_ready = sem("const_ready")
        self.score_ready = sem("score_ready")
        self.score_masked = sem("score_masked")
        self.exp_ready = sem("exp_ready")
        self.share_ready = sem("share_ready")
        self.prob_ready = sem("prob_ready")
        self.probT_ready = sem("probT_ready")
        self.probT_copied = sem("probT_copied")
        self.pair_ready = sem("pair_ready")
        self.pair_copied = sem("pair_copied")
        self.pair_taken = sem("pair_taken")
        self.head_sq = sem("head_sq")
        self.head_ssq = sem("head_ssq")
        self.head_std = sem("head_std")
        self.head_recip = sem("head_recip")
        self.head_done = sem("head_done")
        self.vb_ready = sem("vb_ready")
        self.gelu_ready = sem("gelu_ready")
        self.tok_ready = sem("tok_ready")
        self.tok_copied = sem("tok_copied")
        self.ln_sum = sem("ln_sum")
        self.xc_ready = sem("xc_ready")
        self.ln_sq = sem("ln_sq")
        self.ln_ssq = sem("ln_ssq")
        self.ln_std = sem("ln_std")
        self.xn_ready = sem("xn_ready")
        self.vn_ready = sem("vn_ready")
        self.mix_ready = sem("mix_ready")
        self.mix_taken = sem("mix_taken")
        self.mixed = sem("mixed")
        self.ws_ready = sem("ws_ready")
        self.mask_loaded = sem("mask_loaded")
        self.tri_loaded = sem("tri_loaded")
        self.ws_loaded = sem("ws_loaded")
        self.bs_loaded = sem("bs_loaded")
        self.v_taken = sem("v_taken")
        self.head_copied = sem("head_copied")
        self.was_copied = sem("was_copied")
        self.logit_ready = sem("logit_ready")
        self.kq_ready = sem("kq_ready")
        self.attn_ready = sem("attn_ready")
        self.ks_ready = sem("ks_ready")
        self.ks_turned = sem("ks_turned")
        self.kstok_ready = sem("kstok_ready")
        self.kv_ready = sem("kv_ready")
        self.attn_masked = sem("attn_masked")
        self.state_ready = sem("state_ready")
        self.o_ready = sem("o_ready")
        self.reset_loaded = sem("reset_loaded")
        self.od_mask_loaded = sem("od_mask_loaded")
        self.wa_loaded = sem("wa_loaded")
        self.silu_ready = sem("silu_ready")
        self.abs_ready = sem("abs_ready")
        self.ln_ready = sem("ln_ready")
        self.decay_ready = sem("decay_ready")
        self.left_ready = sem("left_ready")
        self.od_exp = sem("od_exp")
        self.o_copied = sem("o_copied")
        self.od_chain = sem("od_chain")
        self.nsa_free = sem("nsa_free")
        self.pos_loaded = sem("pos_loaded")
        self.sel_loaded = sem("sel_loaded")
        self.b_masks_loaded = sem("b_masks_loaded")
        self.w2_loaded = sem("w2_loaded")
        self.angle_ready = sem("angle_ready")
        self.trig_ready = sem("trig_ready")
        self.kc_taken = sem("kc_taken")
        self.pairs_loaded = sem("pairs_loaded")
        self.gates_turned = sem("gates_turned")
        self.gates_done = sem("gates_done")
        self.gates_taken = sem("gates_taken")
        self.a_ready = sem("a_ready")
        self.a_hi_done = sem("a_hi_done")
        self.a_lo_done = sem("a_lo_done")
        self.cmp_taken = sem("cmp_taken")
        self.cmp_gelu = sem("cmp_gelu")
        self.cmp_turned = sem("cmp_turned")
        self.cmp_hT = sem("cmp_hT")
        self.cmp_out = sem("cmp_out")
        self.cmp_copied = sem("cmp_copied")
        self.kv_taken = sem("kv_taken")
        self.rope_ps = sem("rope_ps")
        self.rope_read = sem("rope_read")
        self.q_taken = sem("q_taken")
        self.half_sq = sem("half_sq")
        self.half_ssq = sem("half_ssq")
        self.half_std = sem("half_std")
        self.half_done = sem("half_done")
        self.conv_done = sem("conv_done")
        self.nsa_step = sem("nsa_step")
        self.gp_copied = sem("gp_copied")
        self.gate_ready = sem("gate_ready")
        self.conv_tap = sem("conv_tap")
        self.conv_sum = sem("conv_sum")
        self.act_ready = sem("act_ready")
        self.val_ready = sem("val_ready")
        self.hid_hi_done = sem("hid_hi_done")
        self.hid_lo_done = sem("hid_lo_done")
        self.w_loaded = [ctx.enter_context(nc.semaphore(f"w_loaded{i}")) for i in range(2)]




def carry(e, c, scalar=False, turn=0):
    if scalar:
        e.activation(c.stat[:, 13:14], c.eps, ACT.Copy)
    else:
        e.memset(c.stat[:, 24 + turn:25 + turn], 0.0)


def chunk_products(pe, n, c, acc, hi, lo, nk, k0=0, start=True, stop=True, wait_k=None, mt=2):
    s = n.chunk % 2
    pe.wait_ge(c.w_lo_done, n(c.w_lo_done))
    for k in range(nk):
        if wait_k is not None:
            pe.wait_ge(wait_k, n(wait_k))
        for m in range(mt):
            w = (c.w_hi[:, s, k, m * P:(m + 1) * P], c.w_lo[:, s, k, m * P:(m + 1) * P])
            r = (hi[:, k0 + k, :], lo[:, k0 + k, :])
            for j, (a, b) in enumerate(((1, 0), (0, 1), (0, 0))):
                last = pe.matmul(acc[:, m, :], w[a], r[b], start=start and k == 0 and j == 0,
                                 stop=stop and k == nk - 1 and j == 2)
    last.then_inc(c.chunk_done, 1)
    n.chunk += 1


def group_slot(pe, n, c):
    if n.group >= 2:
        pe.wait_ge(c.group_taken, n(c.group_taken))
    n.group += 1
    return c.ps[(n.group - 1) % 2]


def sum_squares(pe, n, c):
    n.skip(c.acc_ready, 4)
    pe.wait_ge(c.acc_ready, n(c.acc_ready))
    for j in range(2):
        last = pe.matmul(c.m[0][:, :], c.ones[:, :], c.acc[:, j, :], start=j == 0, stop=j == 1)
    last.then_inc(c.ssq_ready, 1)


def ffn_in_tensor(pe, n, c):
    chunk_products(pe, n, c, group_slot(pe, n, c), c.h_hi, c.h_lo, KT, wait_k=c.h_lo_done)
    sum_squares(pe, n, c)
    chunk_products(pe, n, c, group_slot(pe, n, c), c.h_hi, c.h_lo, KT)

    def pair(e, i):
        for _ in range(2):
            chunk_products(e, n, c, group_slot(e, n, c), c.h_hi, c.h_lo, KT)
    n.loop(pe, FPAIRS - 1, pair)


def ffn_down_tensor(pe, n, c):
    n.skip(c.hid_lo_done, FPAIRS - 1)
    pe.wait_ge(c.hid_lo_done, n(c.hid_lo_done))

    def two_groups(e, i):
        for _ in range(2):
            acc = group_slot(e, n, c)
            for j, nk in enumerate(DOWN_K):
                chunk_products(e, n, c, acc, c.hid_hi, c.hid_lo, nk, 8 * j, j == 0, j == 2)
    n.loop(pe, 2, two_groups)


def out_tensor(pe, n, c):
    def two_groups(e, i):
        for _ in range(2):
            chunk_products(e, n, c, group_slot(e, n, c), c.hid_hi, c.hid_lo, KT)
    chunk_products(pe, n, c, group_slot(pe, n, c), c.hid_hi, c.hid_lo, KT, wait_k=c.hid_lo_done)
    chunk_products(pe, n, c, group_slot(pe, n, c), c.hid_hi, c.hid_lo, KT)
    chunk_products(pe, n, c, group_slot(pe, n, c), c.hid_hi, c.hid_lo, KT)
    chunk_products(pe, n, c, group_slot(pe, n, c), c.hid_hi, c.hid_lo, KT)


def split_next(act, n, c):
    s = n.chunk % 2
    act.wait_ge(c.w_loaded[s], n(c.w_loaded[s], 16))
    if n.chunk >= 2:
        act.wait_ge(c.chunk_done, n(c.chunk_done))
    act.activation(c.w_hi[:, s, :, :].rearrange("p k n -> p (k n)"), c.stage[:, s, :], ACT.Copy)\
        .then_inc(c.w_hi_done, 1)
    n.chunk += 1


def norm_std(act, n, c):
    n.skip(c.acc_ready)
    act.wait_ge(c.ssq_ready, n(c.ssq_ready))
    act.activation(c.rstd[:, :], c.m[0][:, :], ACT.Sqrt, bias=c.eps, scale=1.0 / D)\
        .then_inc(c.std_ready, 1)


def next_h_scalar(act, n, c, m, ready, norm):
    if ready is not None:
        act.wait_ge(ready, n(ready))
    for j in range(2):
        col = PC["norm"] + norm * 8
        act.activation(tile(c.h_hi, 2 * m + j), tile(c.x, 2 * m + j), ACT.Copy,
                       scale=c.par[:, bass.ds(col + 2 * m + j, 1)]).then_inc(c.h_hi_done, 1)
    act.wait_ge(c.acc_ready, n(c.acc_ready))
    carry(act, c, True)
    act.activation(c.sq[:, :, :], two(c.x, m), ACT.Square).then_inc(c.sq_ready, 1)


def ffn_in_scalar(act, n, c, conv):
    def pair(e, i, last=False):
        split_next(e, n, c)
        e.wait_ge(c.gate_ready, n(c.gate_ready))
        if conv is not None:
            for j in range(2):
                f = 2 * i + j
                col = PC["fcw"] + conv * FT * 3
                e.activation(c.sq[:, j, :], c.gate[:, j, 0:T], ACT.Identity,
                             bias=c.par[:, bass.ds(PC["fcb"] + conv * FT + f, 1)],
                             scale=c.par[:, bass.ds(col + f, 1)]).then_inc(c.conv_tap, 1)
            e.wait_ge(c.conv_sum, n(c.conv_sum, 4))
            e.activation(c.sq[:, :, :], c.sq[:, :, :], ACT.Silu).then_inc(c.act_ready, 1)
        else:
            e.activation(c.sq[:, :, :], c.gate[:, :, 2:], ACT.Silu).then_inc(c.act_ready, 1)
        if not last:
            split_next(e, n, c)
        n.skip(c.group_taken, 2)
        e.wait_ge(c.val_ready, n(c.val_ready))
        e.activation(two(c.hid_hi, i), c.val[:, :, :], ACT.Copy).then_inc(c.hid_hi_done, 1)
    split_next(act, n, c)
    norm_std(act, n, c)
    n.loop(act, FPAIRS - 1, pair)
    pair(act, FPAIRS - 1, True)


def result_scalar(act, n, c, chunks, norm, post):
    def one(e, m):
        for _ in range(chunks):
            split_next(e, n, c)
        if post is None:
            next_h_scalar(e, n, c, m, c.group_taken, norm)
        else:
            e.wait_ge(c.group_taken, n(c.group_taken))
            e.wait_ge(c.acc_ready, n(c.acc_ready))
            carry(e, c, True)
            e.activation(c.sq[:, :, :], two(c.y, m), ACT.Square).then_inc(c.sq_ready, 1)

    n.loop(act, 2, lambda e, i: (one(e, 2 * i), one(e, 2 * i + 1)))
    if post is not None:
        norm_std(act, n, c)
        if norm is not None:
            for m in range(4):
                act.wait_ge(c.x_ready, n(c.x_ready))
                for j in range(2):
                    col = PC["norm"] + norm * 8 + 2 * m + j
                    act.activation(c.h_hi[:, 2 * m + j, :], c.x[:, 2 * m + j, :], ACT.Copy,
                                   scale=c.par[:, col:col + 1]).then_inc(c.h_hi_done, 1)
                if m < 2:
                    act.activation((c.sq, c.val)[m][:, :, :], two(c.x, m), ACT.Square)\
                        .then_inc(c.sq_ready, 1)
            n.skip(c.acc_ready)
            for m in (2, 3):
                act.wait_ge(c.acc_ready, n(c.acc_ready))
                act.activation((c.sq, c.val)[m % 2][:, :, :], two(c.x, m), ACT.Square)\
                    .then_inc(c.sq_ready, 1)
            n.skip(c.acc_ready)


def norm_recip(dve, n, c):
    dve.wait_ge(c.std_ready, n(c.std_ready))
    dve.reciprocal(c.rstd[:, :], c.rstd[:, :]).then_inc(c.rstd_ready, 1)
    dve.wait_ge(c.rstd_ready, n(c.rstd_ready))


def add_squares(dve, n, c):
    dve.wait_ge(c.sq_ready, n(c.sq_ready))
    dve.wait_ge(c.acc_ready, n(c.acc_ready))
    dve.tensor_tensor(c.acc[:, :, :], c.acc[:, :, :], c.sq[:, :, :], ALU.add)\
        .then_inc(c.acc_ready, 1)


def clear_squares(dve, n, c):
    dve.memset(c.acc[:, :, :], 0.0).then_inc(c.acc_ready, 1)


def next_h_vector(dve, n, c, m, norm):
    col = PC["norm"] + norm * 8
    for j in range(2):
        dve.wait_ge(c.h_hi_done, n(c.h_hi_done))
        dve.scalar_tensor_tensor(
            tile(c.h_lo, 2 * m + j), tile(c.x, 2 * m + j), c.par[:, bass.ds(col + 2 * m + j, 1)],
            tile(c.h_hi, 2 * m + j).bitcast(F32), ALU.mult, ALU.subtract).then_inc(c.h_lo_done, 1)
    add_squares(dve, n, c)


def ffn_in_vector(dve, n, c, conv):
    rstd = over_tiles(c.rstd[:, :])

    def pair(e, i):
        e.wait_ge(c.chunk_done, n(c.chunk_done))
        e.tensor_tensor(c.gate[:, :, 2:], c.ps[n.group % 2][:, :, :], rstd, ALU.mult)\
            .then_inc(c.group_taken, 1)
        n.group += 1
        e.wait_ge(c.group_taken, n(c.group_taken))
        if conv is not None:
            e.memset(c.gate[:, :, 0:2], 0.0).then_inc(c.gate_ready, 1)
            for j in range(2):
                e.wait_ge(c.conv_tap, n(c.conv_tap))
                for k in (1, 2):
                    col = PC["fcw"] + conv * FT * 3 + k * FT
                    if k == 2:
                        e.wait_ge(c.conv_sum, n(c.conv_sum))
                    e.scalar_tensor_tensor(c.sq[:, j, :], c.gate[:, j, k:k + T],
                                           c.par[:, bass.ds(col + 2 * i + j, 1)], c.sq[:, j, :],
                                           ALU.mult, ALU.add).then_inc(c.conv_sum, 1)
                n.skip(c.conv_sum)
        else:
            e.memset(c.gate[:, :, 0:2], 0.0).then_inc(c.gate_ready, 1)
        e.wait_ge(c.chunk_done, n(c.chunk_done))
        e.tensor_tensor(c.val[:, :, :], c.ps[n.group % 2][:, :, :], rstd, ALU.mult)\
            .then_inc(c.group_taken, 1)
        n.group += 1
        e.wait_ge(c.group_taken, n(c.group_taken))
        e.wait_ge(c.act_ready, n(c.act_ready))
        e.tensor_tensor(c.val[:, :, :], c.val[:, :, :], c.sq[:, :, :], ALU.mult)\
            .then_inc(c.val_ready, 1)
        e.wait_ge(c.val_ready, n(c.val_ready))
        e.wait_ge(c.hid_hi_done, n(c.hid_hi_done))
        e.tensor_tensor(two(c.hid_lo, i), c.val[:, :, :], two(c.hid_hi, i).bitcast(F32),
                        ALU.subtract).then_inc(c.hid_lo_done, 1)
    norm_recip(dve, n, c)
    n.loop(dve, FPAIRS, pair)


def result_vector(dve, n, c, chunks, norm, post):
    clear_squares(dve, n, c)

    def one(e, m):
        n.skip(c.chunk_done, chunks - 1)
        e.wait_ge(c.chunk_done, n(c.chunk_done))
        acc = c.ps[n.group % 2]
        n.group += 1
        if post is None:
            e.tensor_tensor(two(c.x, m), acc[:, :, :], two(c.x, m), ALU.add)\
                .then_inc(c.group_taken, 1)
            e.wait_ge(c.group_taken, n(c.group_taken))
            next_h_vector(e, n, c, m, norm)
        else:
            e.tensor_copy(two(c.y, m), acc[:, :, :]).then_inc(c.group_taken, 1)
            n.skip(c.group_taken)
            add_squares(e, n, c)

    n.loop(dve, 2, lambda e, i: (one(e, 2 * i), one(e, 2 * i + 1)))
    n.skip(c.acc_ready)
    if post is not None:
        norm_recip(dve, n, c)
        if norm is not None:
            clear_squares(dve, n, c)
        rstd = over_tiles(c.rstd[:, :])
        for m in range(6 if norm is not None else 5):
            if m < 4:
                dve.tensor_tensor(two(c.y, m), two(c.y, m), rstd, ALU.mult).then_inc(c.post_y, 1)
            if 1 <= m < 5:
                dve.wait_ge(c.post_y, n(c.post_y))
                for i in (2 * m - 2, 2 * m - 1):
                    col = PC["post"] + post * 8 + i
                    last = dve.scalar_tensor_tensor(c.x[:, i, :], c.y[:, i, :], c.par[:, col:col + 1],
                                                    c.x[:, i, :], ALU.mult, ALU.add)
                last.then_inc(c.x_ready, 1)
            if m >= 2 and norm is not None:
                dve.wait_ge(c.x_ready, n(c.x_ready))
                for i in (2 * m - 4, 2 * m - 3):
                    col = PC["norm"] + norm * 8 + i
                    dve.wait_ge(c.h_hi_done, n(c.h_hi_done))
                    dve.scalar_tensor_tensor(c.h_lo[:, i, :], c.x[:, i, :], c.par[:, col:col + 1],
                                             c.h_hi[:, i, :].bitcast(F32), ALU.mult, ALU.subtract)\
                        .then_inc(c.h_lo_done, 1)
        if norm is not None:
            for m in range(4):
                dve.wait_ge(c.sq_ready, n(c.sq_ready))
                dve.wait_ge(c.acc_ready, n(c.acc_ready))
                dve.tensor_tensor(c.acc[:, :, :], c.acc[:, :, :], (c.sq, c.val)[m % 2][:, :, :], ALU.add)\
                    .then_inc(c.acc_ready, 1)
            n.skip(c.acc_ready)
        else:
            n.skip(c.x_ready, 4)


def final_post_tensor(pe, n, c):
    sum_squares(pe, n, c)


class Unit:

    def __init__(self, q, k, v, mask, out, gate=None, first=True, last=True, keys=P, tiles=1):
        self.q, self.k, self.v, self.mask, self.out = q, k, v, mask, out
        self.gate, self.first, self.last = gate, first, last
        self.tiles, self.keys = tiles, keys
        self.w = keys * tiles


LAG = 2


def attend_tensor(e, n, c, units, ready):
    e.wait_ge(ready, n(ready))
    for u in range(len(units) + LAG + 1):
        if u < len(units):
            x = units[u]
            if u >= 2:
                e.wait_ge(c.score_masked, n(c.score_masked))
            e.matmul(c.m[u % 2][:, 0:x.w], x.q, x.k, start=True, stop=True)\
                .then_inc(c.score_ready, 1)
        v = u - LAG
        if 0 <= v < len(units):
            x = units[v]
            e.wait_ge(c.prob_ready, n(c.prob_ready))
            for j in range(x.tiles):
                last = e.transpose(c.ps[0][0:x.keys, v % 2, j * P:(j + 1) * P],
                                   c.score[:, v % 3, j * x.keys:(j + 1) * x.keys], c.ident[:, :])
            last.then_inc(c.probT_ready, 1)
        v = u - LAG - 1
        if 0 <= v:
            x = units[v]
            e.wait_ge(c.probT_copied, n(c.probT_copied))
            for j in range(x.tiles):
                last = e.matmul(x.out, x.v[j], c.probT[0:x.keys, v % 2, j * P:(j + 1) * P],
                                start=x.first and j == 0, stop=x.last and j == x.tiles - 1)
    last.then_inc(c.pair_ready, 1)
    n.skip(c.score_masked, 2)


def attend_scalar(e, n, c, units):
    for u in range(len(units) + LAG):
        if u < len(units):
            x, b = units[u], u % 3
            e.wait_ge(c.score_masked, n(c.score_masked))
            e.activation(c.score[:, b, 0:x.w], c.score[:, b, 0:x.w], ACT.Exp,
                         bias=c.stat[:, b:b + 1], scale=-1.0,
                         accum_out=c.stat[:, 4 + b:5 + b]).then_inc(c.exp_ready, 1)
        v = u - LAG
        if v >= 0:
            x, b = units[v], v % 2
            e.wait_ge(c.probT_ready, n(c.probT_ready))
            e.activation(c.probT[0:x.keys, b, 0:x.tiles * P], c.ps[0][0:x.keys, b, 0:x.tiles * P],
                         ACT.Copy).then_inc(c.probT_copied, 1)


def attend_vector(e, n, c, units, scale):
    for u in range(len(units) + 1):
        if u < len(units):
            x, b = units[u], u % 3
            e.wait_ge(c.score_ready, n(c.score_ready))
            carry(e, c, turn=1 + u % 4)
            e.tensor_tensor_reduce(c.score[:, b, 0:x.w], c.m[u % 2][:, 0:x.w], x.mask, -scale, 3e38,
                                   ALU.add, ALU.min, c.stat[:, b:b + 1]).then_inc(c.score_masked, 1)
        if u >= 1:
            x, b = units[u - 1], (u - 1) % 3
            e.wait_ge(c.exp_ready, n(c.exp_ready))
            e.reciprocal(c.stat[:, 16 + b:17 + b], c.stat[:, 4 + b:5 + b]).then_inc(c.share_ready, 1)
            e.wait_ge(c.share_ready, n(c.share_ready))
            p, share = c.score[:, b, 0:x.w], c.stat[:, 16 + b:17 + b]
            if x.gate is None:
                e.tensor_scalar(p, p, share, None, ALU.mult).then_inc(c.prob_ready, 1)
            else:
                e.tensor_scalar(p, p, share, x.gate, ALU.mult, ALU.mult).then_inc(c.prob_ready, 1)


EVEN_SCALE = HD ** -0.5


def even_units(c):
    units = []
    for hh in range(2):
        r = slice(HD * hh, HD * hh + HD)
        for i in range(TT):
            units.append(Unit(c.qs[r, i * P:(i + 1) * P], c.ks[r, 0:(i + 1) * P],
                              [c.vs[:, j, r] for j in range(i + 1)], c.ev_mask[:, 384 - P * i:T],
                              c.m[3][r, i * P:(i + 1) * P], tiles=i + 1))
    return units


def even_tensor(pe, n, c, norm):
    pe.wait_ge(c.ones_loaded, 16)
    pe.wait_ge(c.blockones_loaded, 16)
    pe.wait_ge(c.ident_loaded, 16)

    def z(e, **kw):
        chunk_products(e, n, c, group_slot(e, n, c), c.h_hi, c.h_lo, KT, **kw)

    def head_norm():
        pe.wait_ge(c.head_sq, n(c.head_sq))
        for j in range(2):
            last = pe.matmul(c.m[1 + j][:, :], c.blockones[:, :], c.sq[:, j, :], start=True, stop=True)
        last.then_inc(c.head_ssq, 1)

    z(pe, wait_k=c.h_lo_done)
    sum_squares(pe, n, c)
    for j in range(4):
        z(pe)
        head_norm()
    z(pe)
    n.loop(pe, 2, lambda e, i: (z(e), z(e)))
    n.skip(c.group_taken, 0)
    for t in range(TT):
        if t >= 2:
            pe.wait_ge(c.tok_copied, n(c.tok_copied))
        else:
            pe.wait_ge(c.vb_ready, n(c.vb_ready))
        for k in range(4):
            last = pe.transpose(c.m[1 + t % 2][:, k * P:(k + 1) * P], c.ev_vb[:, k, t * P:(t + 1) * P],
                                c.ident[:, :])
        last.then_inc(c.tok_ready, 1)
    pe.wait_ge(c.tok_copied, n(c.tok_copied, 2))
    pe.wait_ge(c.gelu_ready, n(c.gelu_ready, 2))
    for k in range(4):
        last = pe.matmul(c.m[1][:, :], c.ones[:, :], c.ev_v[:, k, :], start=k == 0, stop=k == 3)
    last.then_inc(c.ln_sum, 1)
    for k in range(4):
        if k % 2 == 0:
            pe.wait_ge(c.ln_sq, n(c.ln_sq))
        sq = c.sq if k < 2 else c.val
        last = pe.matmul(c.m[2][:, :], c.ones[:, :], sq[:, k % 2, :], start=k == 0, stop=k == 3)
    last.then_inc(c.ln_ssq, 1)
    pe.wait_ge(c.vn_ready, n(c.vn_ready, 4))
    for t in range(TT):
        if t >= 2:
            pe.wait_ge(c.tok_copied, n(c.tok_copied))
        for k in range(4):
            last = pe.transpose(c.m[1 + t % 2][:, k * P:(k + 1) * P], c.ev_v[:, k, t * P:(t + 1) * P],
                                c.ident[:, :])
        last.then_inc(c.tok_ready, 1)
    pe.wait_ge(c.tok_copied, n(c.tok_copied, 2))
    pe.wait_ge(c.ws_ready, n(c.ws_ready))
    for m in range(4):
        bank = c.m[m % 2 * 3]
        if m >= 2:
            pe.wait_ge(c.mix_taken, n(c.mix_taken))
        for hh in range(2):
            g = 2 * m + hh
            for t in range(TT):
                last = pe.matmul(bank[HD * hh:HD * hh + HD, t * P:(t + 1) * P],
                                 c.ev_vntok[:, t, g * HD:(g + 1) * HD], c.ev_ws[:, g, :],
                                 start=True, stop=True)
        last.then_inc(c.mix_ready, 1)
    pe.wait_ge(c.mix_taken, n(c.mix_taken, 2))
    n.loop(pe, 4, lambda e, m: attend_tensor(e, n, c, even_units(c), c.pair_copied))
    out_tensor(pe, n, c)


def even_scalar(act, n, c, norm, a, out):
    act.dma_start(c.ev_mask[:, :], a["ev_mask"]).then_inc(c.mask_loaded, 16)
    act.dma_start(c.tri[:, :], a["tri"]).then_inc(c.tri_loaded, 16)
    act.dma_start(c.ev_ws[:, :, :], a["ev_ws"]).then_inc(c.ws_loaded, 16)

    def square(j):
        act.wait_ge(c.group_taken, n(c.group_taken))
        act.activation(c.sq[:, :, :], c.ev_qk[:, 2 * j:2 * j + 2, :], ACT.Square)\
            .then_inc(c.head_sq, 1)

    def std(j):
        act.wait_ge(c.head_ssq, n(c.head_ssq))
        if j >= 1:
            act.wait_ge(c.head_done, n(c.head_done))
        for k in range(2):
            act.activation(c.val[:, k, :], c.m[1 + k][:, :], ACT.Sqrt, bias=c.eps, scale=1.0 / HD)\
                .then_inc(c.head_std, 1)

    split_next(act, n, c)
    norm_std(act, n, c)
    square(0)
    for j in range(1, 4):
        split_next(act, n, c)
        std(j - 1)
        square(j)
    split_next(act, n, c)
    std(3)
    split_next(act, n, c)
    n.skip(c.group_taken, 2)
    for j in range(4):
        split_next(act, n, c)
        act.wait_ge(c.group_taken, n(c.group_taken))
        g = (c.ev_v if j < 2 else c.ev_u)[:, 2 * (j % 2):2 * (j % 2) + 2, :]
        act.activation(g, g, ACT.Gelu).then_inc(c.gelu_ready, 1)
        if j == 3:
            for t in range(TT):
                act.wait_ge(c.tok_ready, n(c.tok_ready))
                act.activation(c.ev_vtok[:, t, :], c.m[1 + t % 2][:, :], ACT.Copy)\
                    .then_inc(c.tok_copied, 1)
    act.dma_start(c.ev_bs[:, :, :], a["ev_bs"]).then_inc(c.bs_loaded, 16)
    for j in range(2):
        act.wait_ge(c.xc_ready, n(c.xc_ready))
        act.activation((c.sq, c.val)[j][:, :, :], c.ev_v[:, 2 * j:2 * j + 2, :], ACT.Square)\
            .then_inc(c.ln_sq, 1)
    act.wait_ge(c.ln_ssq, n(c.ln_ssq))
    act.activation(c.gate[:, 0, 0:T], c.m[2][:, :], ACT.Sqrt, bias=c.eps, scale=1.0 / 512)\
        .then_inc(c.ln_std, 1)
    for k in range(4):
        if k % 2 == 0:
            act.wait_ge(c.xn_ready, n(c.xn_ready))
        act.activation(c.ev_v[:, k, :], c.ev_v[:, k, :], ACT.Identity,
                       bias=c.par[:, PC["lnb"] + k:PC["lnb"] + k + 1],
                       scale=c.par[:, PC["lng"] + k:PC["lng"] + k + 1]).then_inc(c.vn_ready, 1)
    for t in range(TT):
        act.wait_ge(c.tok_ready, n(c.tok_ready))
        act.activation(c.ev_vntok[:, t, :], c.m[1 + t % 2][:, :], ACT.Copy).then_inc(c.tok_copied, 1)
    for m in range(4):
        act.wait_ge(c.mixed, n(c.mixed))
        act.activation(c.hid_hi[:, m, :], c.ev_u[:, m, :], ACT.Copy).then_inc(c.hid_hi_done, 1)
    n.loop(act, 4, lambda e, m: attend_scalar(e, n, c, even_units(c)))
    for m in range(4):
        if m == 0:
            act.wait_ge(c.pair_taken, n(c.pair_taken, 4))
        act.activation(c.hid_hi[:, 4 + m, :], c.ev_qk[:, m, :], ACT.Copy).then_inc(c.hid_hi_done, 1)
    result_scalar(act, n, c, 1, norm, None)


def hid_low(e, n, c, m, src):
    e.wait_ge(c.hid_hi_done, n(c.hid_hi_done))
    e.tensor_tensor(c.hid_lo[:, m, :], src, c.hid_hi[:, m, :].bitcast(F32), ALU.subtract)\
        .then_inc(c.hid_lo_done, 1)


def even_vector(dve, n, c, norm):
    rstd = over_tiles(c.rstd[:, :])

    def take(dst):
        dve.wait_ge(c.chunk_done, n(c.chunk_done))
        dve.tensor_tensor(dst, c.ps[n.group % 2][:, :, :], rstd, ALU.mult).then_inc(c.group_taken, 1)
        n.group += 1
        n.skip(c.group_taken)

    def finish(j):
        dve.wait_ge(c.head_std, n(c.head_std, 2))
        dve.reciprocal(c.val[:, :, :], c.val[:, :, :]).then_inc(c.head_recip, 1)
        dve.wait_ge(c.head_recip, n(c.head_recip))
        dve.wait_ge(c.group_taken, n(c.group_taken, 0))
        for k in range(2):
            col = PC["qkg"] + j // 2
            t = c.ev_qk[:, 2 * j + k, :]
            last = dve.scalar_tensor_tensor(t, t, c.par[:, col:col + 1], c.val[:, k, :],
                                            ALU.mult, ALU.mult)
        last.then_inc(c.head_done, 1)
        n.skip(c.head_done)

    norm_recip(dve, n, c)
    dve.wait_ge(c.tri_loaded, 16)
    dve.wait_ge(c.ws_loaded, 16)
    dve.tensor_tensor(c.ev_ws[:, :, :], c.ev_ws[:, :, :], over_tiles(c.tri[:, :], 8), ALU.mult)\
        .then_inc(c.ws_ready, 1)
    take(c.ev_qk[:, 0:2, :])
    for j in range(1, 4):
        take(c.ev_qk[:, 2 * j:2 * j + 2, :])
        finish(j - 1)
    take(c.ev_vb[:, 0:2, :])
    finish(3)
    take(c.ev_vb[:, 2:4, :])
    dve.wait_ge(c.group_taken, n(c.group_taken, 0))
    for k in range(2):
        dve.memset(c.stat[:, 8 + k:9 + k], 0.0).then_inc(c.vb_ready, 1)
    for g in (c.ev_v, c.ev_u):
        for j in range(2):
            take(g[:, 2 * j:2 * j + 2, :])
    dve.wait_ge(c.ln_sum, n(c.ln_sum))
    for j in range(2):
        v = c.ev_v[:, 2 * j:2 * j + 2, :]
        dve.scalar_tensor_tensor(v, over_tiles(c.m[1][:, :]), -1.0 / 512, v, ALU.mult, ALU.add)\
            .then_inc(c.xc_ready, 1)
    dve.wait_ge(c.ln_std, n(c.ln_std))
    dve.reciprocal(c.gate[:, 0, 0:T], c.gate[:, 0, 0:T]).then_inc(c.head_recip, 1)
    dve.wait_ge(c.head_recip, n(c.head_recip))
    for j in range(2):
        v = c.ev_v[:, 2 * j:2 * j + 2, :]
        dve.tensor_tensor(v, v, over_tiles(c.gate[:, 0, 0:T]), ALU.mult).then_inc(c.xn_ready, 1)
    dve.wait_ge(c.bs_loaded, 16)
    dve.wait_ge(c.gelu_ready, n(c.gelu_ready, 4))
    for m in range(4):
        dve.wait_ge(c.mix_ready, n(c.mix_ready))
        bank = c.m[m % 2 * 3][:, :].rearrange("p (t s) -> p t s", t=TT)
        dve.tensor_tensor(c.val[:, m % 2, :].rearrange("p (t s) -> p t s", t=TT), bank,
                          over_tiles(c.ev_bs[:, m, :], TT), ALU.add).then_inc(c.mix_taken, 1)
        dve.wait_ge(c.mix_taken, n(c.mix_taken))
        dve.tensor_tensor(c.ev_u[:, m, :], c.val[:, m % 2, :], c.ev_u[:, m, :], ALU.mult)\
            .then_inc(c.mixed, 1)
        dve.wait_ge(c.mixed, n(c.mixed))
        hid_low(dve, n, c, m, c.ev_u[:, m, :])
    dve.wait_ge(c.mask_loaded, 16)
    dve.wait_ge(c.tok_copied, n(c.tok_copied, 4))
    n.skip(c.tok_copied, 4)

    def pair(e, m):
        e.tensor_copy(c.qs[:, :], tile(c.ev_qk, m))
        e.tensor_copy(c.ks[:, :], tile(c.ev_qk, m + 4))
        e.tensor_copy(c.vs[:, :, :], c.ev_vtok[:, :, bass.ds(m * P, P)]).then_inc(c.pair_copied, 1)
        attend_vector(e, n, c, even_units(c), EVEN_SCALE)
        e.wait_ge(c.pair_ready, n(c.pair_ready))
        carry(e, c)
        e.tensor_copy(tile(c.ev_qk, m), c.m[3][:, :]).then_inc(c.pair_taken, 1)
    n.loop(dve, 4, pair)
    dve.wait_ge(c.pair_taken, n(c.pair_taken, 4))
    for m in range(4):
        hid_low(dve, n, c, 4 + m, c.ev_qk[:, m, :])
    result_vector(dve, n, c, 1, norm, None)


C_HEADS = 4
C_CHUNK = 64
N_CH = T // C_CHUNK
TAU = 16.0


def kv_bank(c, j):
    return c.ps[j % 2][:, j // 4, j // 2 % 2 * CW:(j // 2 % 2 + 1) * CW]


def odd_tensor(pe, n, c, norm):
    def z(e, **kw):
        chunk_products(e, n, c, group_slot(e, n, c), c.h_hi, c.h_lo, KT, **kw)

    z(pe, wait_k=c.h_lo_done, mt=1)
    sum_squares(pe, n, c)
    n.loop(pe, 2, lambda e, i: (z(e), z(e)))

    def values(e, i):
        for _ in range(2):
            e.wait_ge(c.was_copied, n(c.was_copied))
            e.matmul(c.m[0][:, :], c.od_was[0:16, :], c.od_ga[0:16, :], start=True, stop=True)\
                .then_inc(c.logit_ready, 1)
            z(e)
            e.wait_ge(c.ks_ready, n(c.ks_ready))
            for t in range(TT):
                last = e.transpose(c.m[3][:, t * P:(t + 1) * P], c.od_e3[:, t * P:(t + 1) * P],
                                   c.ident[:, :])
            last.then_inc(c.ks_turned, 1)
            e.wait_ge(c.v_taken, n(c.v_taken))
            for t in range(TT):
                for k in range(2):
                    last = e.transpose(c.m[1 + t // 2][:, (t % 2) * CW + k * P:(t % 2) * CW + (k + 1) * P],
                                       c.val[:, k, t * P:(t + 1) * P], c.ident[:, :])
            last.then_inc(c.tok_ready, 1)
    n.loop(pe, 2, values)
    n.skip(c.tok_copied, 8)
    n.loop(pe, 2, lambda e, i: (z(e), z(e)))

    def square_sum(e):
        e.wait_ge(c.head_sq, n(c.head_sq))
        for k in range(2):
            last = e.matmul(c.m[1][:, :], c.ones[:, :], c.sq[:, k, :], start=k == 0, stop=k == 1)
        last.then_inc(c.head_ssq, 1)

    def head(e, h, first=False):
        e.wait_ge(c.head_copied, n(c.head_copied))
        for t in range(TT):
            last = e.matmul(c.m[0][:, t * P:(t + 1) * P], c.od_kt[:, t * P:(t + 1) * P],
                            c.od_qt[:, t * P:(t + 1) * P], start=True, stop=True)
        last.then_inc(c.attn_ready, 1)
        for j in range(N_CH - 1):
            r = slice(C_CHUNK * (j % 2), C_CHUNK * (j % 2) + C_CHUNK)
            last = e.matmul(kv_bank(c, j),
                            c.od_kstok[r, j // 2, :], c.od_vs[r, j // 2, :], start=True, stop=True)
        last.then_inc(c.kv_ready, 1)
        if not first:
            square_sum(e)
        e.wait_ge(c.attn_masked, n(c.attn_masked))
        e.wait_ge(c.state_ready, n(c.state_ready, N_CH - 1))
        for k in range(2):
            bank = c.m[(3, 2)[k]]
            for t in range(TT):
                e.matmul(bank[:, t * P:(t + 1) * P], c.od_vs[:, t, k * P:(k + 1) * P],
                         c.od_at[:, t, :], start=True, stop=False)
                for j in (2 * t, 2 * t + 1):
                    if j == 0:
                        continue
                    last = e.matmul(bank[:, j * C_CHUNK:(j + 1) * C_CHUNK],
                                    c.od_state[:, j, k * P:(k + 1) * P],
                                    c.od_qt[:, j * C_CHUNK:(j + 1) * C_CHUNK],
                                    start=False, stop=j == 2 * t + 1)
        last.then_inc(c.o_ready, 1)
    head(pe, 0, True)
    n.loop(pe, C_HEADS - 1, lambda e, i: head(e, i + 1))
    square_sum(pe)
    out_tensor(pe, n, c)


def odd_scalar(act, n, c, norm, a, out):
    act.dma_start(c.od_reset[:, :], a["od_reset"]).then_inc(c.reset_loaded, 16)
    act.dma_start(c.od_mask[:, :], a["od_mask"]).then_inc(c.od_mask_loaded, 16)
    act.dma_start(c.od_wa[0:16, :], a["od_wa"]).then_inc(c.wa_loaded, 16)
    split_next(act, n, c)
    norm_std(act, n, c)
    n.loop(act, 2, lambda e, i: (split_next(e, n, c), split_next(e, n, c)))

    def front(e, h):
        bias = c.par[:, bass.ds(PC["ba"] + h, 1)]
        e.wait_ge(c.logit_ready, n(c.logit_ready))
        e.activation(c.od_t1[:, :], c.m[0][:, :], ACT.Abs, bias=bias).then_inc(c.abs_ready, 1)
        e.wait_ge(c.abs_ready, n(c.abs_ready))
        e.activation(c.od_t1[:, :], c.od_t1[:, :], ACT.Exp, scale=-1.0).then_inc(c.abs_ready, 1)
        e.wait_ge(c.abs_ready, n(c.abs_ready))
        e.activation(c.od_t1[:, :], c.od_t1[:, :], ACT.Ln, bias=c.one).then_inc(c.ln_ready, 1)
        e.wait_ge(c.decay_ready, n(c.decay_ready))
        e.activation(c.od_e1[:, :], c.od_b[:, :], ACT.Exp, scale=1.0 / TAU).then_inc(c.od_exp, 1)
        e.activation(c.od_e2[:, :], c.od_b[:, :], ACT.Exp, scale=-1.0 / TAU).then_inc(c.od_exp, 1)
        e.wait_ge(c.left_ready, n(c.left_ready))
        e.activation(c.od_e3[:, :], c.od_e3[:, :], ACT.Exp, scale=1.0 / TAU).then_inc(c.od_exp, 1)
        e.wait_ge(c.ks_turned, n(c.ks_turned))
        e.activation(tile(c.od_kstoks, h), c.m[3][:, :], ACT.Copy).then_inc(c.kstok_ready, 1)

    def values(e, i):
        for s in range(2):
            split_next(e, n, c)
            front(e, 2 * i + s)
            e.wait_ge(c.tok_ready, n(c.tok_ready))
            for b in range(2):
                e.activation(c.od_vtok[:, 2 * b:2 * b + 2, bass.ds((2 * i + s) * CW, CW)],
                             c.m[1 + b][:, :].rearrange("p (t f) -> p t f", t=2), ACT.Copy)\
                    .then_inc(c.tok_copied, 1)
    n.loop(act, 2, values)
    n.skip(c.group_taken, 9)

    def gates(e, i):
        for s in range(2):
            split_next(e, n, c)
            e.wait_ge(c.group_taken, n(c.group_taken))
            e.activation(two(c.od_r, 2 * i + s), two(c.od_r, 2 * i + s), ACT.Silu)\
                .then_inc(c.silu_ready, 1)
    n.loop(act, 2, gates)

    def tail(e, h):
        e.wait_ge(c.head_ssq, n(c.head_ssq))
        e.activation(c.od_std[:, :], c.m[1][:, :], ACT.Sqrt, bias=c.eps, scale=1.0 / CW)\
            .then_inc(c.head_std, 1)
        e.wait_ge(c.mixed, n(c.mixed))
        e.activation(two(c.hid_hi, h), c.val[:, :, :], ACT.Copy).then_inc(c.hid_hi_done, 1)

    def squares(e):
        e.wait_ge(c.o_copied, n(c.o_copied))
        e.activation(c.sq[:, :, :], c.val[:, :, :], ACT.Square).then_inc(c.head_sq, 1)

    squares(act)
    n.loop(act, C_HEADS - 1, lambda e, i: (tail(e, i), squares(e)))
    tail(act, C_HEADS - 1)
    result_scalar(act, n, c, 1, norm, None)


def odd_vector(dve, n, c, norm):
    def take(e, dst, rstd=None, part=P, mt=2):
        e.wait_ge(c.chunk_done, n(c.chunk_done))
        r = over_tiles(c.rstd[0:part, :], mt)
        e.tensor_tensor(dst, c.ps[n.group % 2][0:part, 0:mt, :], r, ALU.mult)\
            .then_inc(c.group_taken, 1)
        n.group += 1
        n.skip(c.group_taken)

    norm_recip(dve, n, c)
    dve.memset(c.od_at[:, :, :], 0.0)
    take(dve, c.od_ga[0:16, :].unsqueeze(1), part=16, mt=1)
    for t in (c.od_q, c.od_k):
        for j in range(2):
            take(dve, t[:, 2 * j:2 * j + 2, :])

    dve.wait_ge(c.reset_loaded, 16)
    dve.wait_ge(c.wa_loaded, 16)
    by_chunk = "p (j s) -> p j s"

    def front(e, h):
        e.tensor_copy(c.od_was[0:16, :], c.od_wa[0:16, bass.ds(h * P, P)]).then_inc(c.was_copied, 1)
        e.wait_ge(c.logit_ready, n(c.logit_ready))
        e.wait_ge(c.ln_ready, n(c.ln_ready))
        e.tensor_scalar(c.od_t2[:, :], c.m[0][:, :], c.par[:, bass.ds(PC["ba"] + h, 1)], 0.0,
                        ALU.add, ALU.min).then_inc(c.od_chain, 1)
        e.wait_ge(c.od_chain, n(c.od_chain))
        e.tensor_tensor(c.od_t2[:, :], c.od_t2[:, :], c.od_t1[:, :], ALU.subtract).then_inc(c.od_chain, 1)
        e.wait_ge(c.od_chain, n(c.od_chain))
        e.tensor_tensor_scan(c.od_b[:, :], c.od_reset[:, :], c.od_t2[:, :], 0.0, ALU.mult, ALU.add)\
            .then_inc(c.decay_ready, 1)
        e.wait_ge(c.decay_ready, n(c.decay_ready))
        b = c.od_b[:, :].rearrange(by_chunk, j=N_CH)
        e.tensor_tensor(c.od_e3[:, :].rearrange(by_chunk, j=N_CH),
                        b[:, :, C_CHUNK - 1:C_CHUNK].to_broadcast([P, N_CH, C_CHUNK]), b, ALU.subtract)\
            .then_inc(c.left_ready, 1)
        e.wait_ge(c.od_exp, n(c.od_exp))
        e.scalar_tensor_tensor(tile(c.od_q, h), tile(c.od_q, h), float(P) ** -0.5, c.od_e1[:, :],
                               ALU.mult, ALU.mult)
        e.tensor_copy(tile(c.od_decays, h),
                      c.od_e1[:, :].rearrange(by_chunk, j=N_CH)[:, :, C_CHUNK - 1:C_CHUNK]
                      .rearrange("p j o -> p (j o)"))
        e.wait_ge(c.od_exp, n(c.od_exp, 2))
        e.tensor_tensor(c.od_e3[:, :], tile(c.od_k, h), c.od_e3[:, :], ALU.mult).then_inc(c.ks_ready, 1)
        e.wait_ge(c.ks_ready, n(c.ks_ready))
        e.tensor_tensor(tile(c.od_k, h), tile(c.od_k, h), c.od_e2[:, :], ALU.mult)\
            .then_inc(c.kq_ready, 1)

    def values(e, i):
        for s in range(2):
            front(e, 2 * i + s)
            take_v(e)
            e.wait_ge(c.kstok_ready, n(c.kstok_ready))

    def take_v(e):
        e.wait_ge(c.chunk_done, n(c.chunk_done))
        e.tensor_tensor(c.val[:, :, :], c.ps[n.group % 2][:, :, :], over_tiles(c.rstd[:, :]), ALU.mult)\
            .then_inc(c.group_taken, 1)
        n.group += 1
        n.skip(c.group_taken)
        e.wait_ge(c.group_taken, n(c.group_taken, 0))
        e.memset(c.stat[:, 8:9], 0.0).then_inc(c.v_taken, 1)
        e.wait_ge(c.tok_copied, n(c.tok_copied, 2))
    n.loop(dve, 2, values)
    n.loop(dve, 2, lambda e, i: (take(e, two(c.od_r, 2 * i)), take(e, two(c.od_r, 2 * i + 1))))
    dve.wait_ge(c.od_mask_loaded, 16)
    dve.wait_ge(c.silu_ready, n(c.silu_ready, 4))
    dve.wait_ge(c.group_taken, n(c.group_taken, 0))
    dve.wait_ge(c.kq_ready, n(c.kq_ready, 4))

    def head(e, h, first=False):
        if not first:
            e.wait_ge(c.o_copied, n(c.o_copied))
            carry(e, c)
        e.tensor_copy(c.od_qt[:, :], tile(c.od_q, h))
        e.tensor_copy(c.od_kt[:, :], tile(c.od_k, h))
        e.tensor_copy(c.od_kstok[:, :, :].rearrange("p t k -> p (t k)"), tile(c.od_kstoks, h))
        e.tensor_copy(c.od_decay[:, :], tile(c.od_decays, h))
        e.tensor_copy(c.od_vs[:, :, :], c.od_vtok[:, :, bass.ds(h * CW, CW)]).then_inc(c.head_copied, 1)
        e.wait_ge(c.attn_ready, n(c.attn_ready))
        carry(e, c, turn=1)
        e.copy_predicated(c.od_at[:, :, :], over_tiles(c.od_mask[:, :], TT),
                          c.m[0][:, :].rearrange("p (t s) -> p t s", t=TT)).then_inc(c.attn_masked, 1)
        e.wait_ge(c.kv_ready, n(c.kv_ready))
        for j in range(N_CH - 1):
            kv = kv_bank(c, j)
            if j == 0:
                e.tensor_copy(c.od_state[:, 1, :], kv).then_inc(c.state_ready, 1)
            else:
                e.wait_ge(c.state_ready, n(c.state_ready))
                e.scalar_tensor_tensor(c.od_state[:, j + 1, :], c.od_state[:, j, :],
                                       c.od_decay[:, j:j + 1], kv, ALU.mult, ALU.add)\
                    .then_inc(c.state_ready, 1)
        n.skip(c.state_ready)

    def tail(e, h):
        e.wait_ge(c.head_std, n(c.head_std))
        e.reciprocal(c.od_std[:, :], c.od_std[:, :]).then_inc(c.od_chain, 1)
        e.wait_ge(c.od_chain, n(c.od_chain))
        e.tensor_tensor(c.val[:, :, :], c.val[:, :, :], over_tiles(c.od_std[:, :]), ALU.mult)\
            .then_inc(c.od_chain, 1)
        e.wait_ge(c.od_chain, n(c.od_chain))
        for k in range(2):
            last = e.scalar_tensor_tensor(c.val[:, k, :], c.val[:, k, :],
                                          c.par[:, PC["hg"] + k:PC["hg"] + k + 1],
                                          tile(c.od_r, 2 * h + k), ALU.mult, ALU.mult)
        last.then_inc(c.mixed, 1)
        e.wait_ge(c.mixed, n(c.mixed))
        e.wait_ge(c.hid_hi_done, n(c.hid_hi_done))
        for k in range(2):
            e.tensor_tensor(tile(c.hid_lo, 2 * h + k), c.val[:, k, :],
                            tile(c.hid_hi, 2 * h + k).bitcast(F32), ALU.subtract)\
                .then_inc(c.hid_lo_done, 1)

    def output(e):
        e.wait_ge(c.o_ready, n(c.o_ready))
        for k in range(2):
            last = e.tensor_copy(c.val[:, k, :], c.m[(3, 2)[k]][:, :])
        last.then_inc(c.o_copied, 1)

    head(dve, 0, True)
    output(dve)

    def step(e, i):
        head(e, i + 1)
        tail(e, i)
        e.memset(c.stat[:, 8:9], 0.0).then_inc(c.od_chain, 1)
        e.wait_ge(c.od_chain, n(c.od_chain))
        output(e)
    n.loop(dve, C_HEADS - 1, step)
    dve.wait_ge(c.o_copied, n(c.o_copied))
    tail(dve, C_HEADS - 1)
    result_vector(dve, n, c, 1, norm, None)


N_CMP = 31
BOTH = 2 * N_CMP
NSA_SCALE = HD ** -0.5
TWO_PI = (6.28125, 0.0019350051879882812, 3.0199159819e-07)
ROUND = 12582912.0


def nsa_units(c, g):
    units = []
    for hh in range(2):
        r = slice(HD * hh, HD * hh + HD)
        kv = slice(HD * g, HD * g + HD)
        for i in range(TT):
            out = c.m[3][r, i * P:(i + 1) * P]
            gate = [c.gp[:, i * 6 + hh * 3 + b:i * 6 + hh * 3 + b + 1] for b in range(3)]
            units.append(Unit(c.qs[r, i * P:(i + 1) * P], c.b_kc[r, g * N_CMP:(g + 1) * N_CMP],
                              [c.b_vc[0:N_CMP, g, :]], c.b_cmask[:, i, 0:N_CMP], out, gate[0],
                              last=False, keys=N_CMP))
            for b, k in ((0, c.b_ks), (1, c.b_kw)):
                units.append(Unit(c.qs2[r, i * P:(i + 1) * P], k[r, g, 0:(i + 1) * P],
                                  [c.b_vs[:, b, j, kv] for j in range(i + 1)],
                                  c.b_mask[:, 384 - P * i:T], out, gate[1 + b], first=False,
                                  last=b == 1, tiles=i + 1))
    return units


def nsa_tensor(pe, n, c, l, norm, post):
    def z(**kw):
        chunk_products(pe, n, c, group_slot(pe, n, c), c.h_hi, c.h_lo, KT, **kw)

    def compressed(kv):
        acc = group_slot(pe, n, c)
        pe.wait_ge(c.a_lo_done, n(c.a_lo_done))
        for half in range(2):
            s = n.chunk % 2
            pe.wait_ge(c.w_lo_done, n(c.w_lo_done))
            for k in range(KT):
                j = KT * half + k
                x = [t[:, kv, j * BOTH:(j + 1) * BOTH] for t in (c.b_a_hi, c.b_a_lo)]
                w = [t[:, s, k, :] for t in (c.w_hi, c.w_lo)]
                for q, (a, b) in enumerate(((1, 0), (0, 1), (0, 0))):
                    last = pe.matmul(acc[0:BOTH, 0, 0:CW], x[a], w[b], start=j == 0 and q == 0,
                                     stop=j == 15 and q == 2)
            last.then_inc(c.chunk_done, 1)
            n.chunk += 1

    def compressed_out(kv):
        pe.wait_ge(c.cmp_gelu, n(c.cmp_gelu))
        for k in range(2):
            last = pe.transpose(c.m[3][:, k * 64:k * 64 + BOTH], c.b_h[0:BOTH, k * P:(k + 1) * P],
                                c.ident[0:BOTH, 0:BOTH])
        last.then_inc(c.cmp_turned, 1)
        pe.wait_ge(c.cmp_hT, n(c.cmp_hT))
        if kv == 0:
            for k in range(2):
                last = pe.matmul(c.m[3][:, 0:BOTH], c.b_w2k[:, k, :], c.b_hT[:, k, 0:BOTH],
                                 start=k == 0, stop=k == 1)
        else:
            for g in range(2):
                for k in range(2):
                    last = pe.matmul(c.m[3][0:N_CMP, g * HD:(g + 1) * HD],
                                     c.b_hT[:, k, g * N_CMP:(g + 1) * N_CMP], c.b_w2v[:, k, :],
                                     start=k == 0, stop=k == 1)
        last.then_inc(c.cmp_out, 1)
        pe.wait_ge(c.cmp_copied, n(c.cmp_copied))

    def rope_k(b):
        src = (c.val, c.b_y)[b]
        pe.wait_ge(c.kv_taken, n(c.kv_taken))
        for g in range(2):
            for j in range(2):
                last = pe.matmul(c.m[1 + j][:, :], c.b_sel[:, 2 * g + j, :], src[:, 0, :],
                                 start=True, stop=True)
            last.then_inc(c.rope_ps, 1)
            if g == 0:
                for t in range(TT):
                    last = pe.transpose(c.m[3][:, t * P:(t + 1) * P], src[:, 1, t * P:(t + 1) * P],
                                        c.ident[:, :])
                last.then_inc(c.tok_ready, 1)
            pe.wait_ge(c.rope_read, n(c.rope_read))
        pe.wait_ge(c.tok_copied, n(c.tok_copied))

    def rope_q(j):
        for k in range(2):
            last = pe.matmul(c.m[1 + k][:, :], c.b_sel[:, 4, :], c.b_q[:, 2 * j + k, :],
                             start=True, stop=True)
        last.then_inc(c.rope_ps, 1)
        pe.wait_ge(c.rope_read, n(c.rope_read))

    z(wait_k=c.h_lo_done)
    sum_squares(pe, n, c)
    z()
    z()
    pe.wait_ge(c.sel_loaded, 16 * (l + 1))
    rope_k(0)
    z(mt=1)
    rope_k(1)
    z()
    pe.wait_ge(c.gates_taken, n(c.gates_taken))
    for t in range(TT):
        last = pe.transpose(c.m[3][:, t * 24:(t + 1) * 24], c.acc[0:24, 0, t * P:(t + 1) * P],
                            c.ident[0:24, 0:24])
    last.then_inc(c.gates_turned, 1)
    z()
    pe.wait_ge(c.q_taken, n(c.q_taken))
    rope_q(0)
    pe.wait_ge(c.gates_done, n(c.gates_done))
    compressed(0)
    pe.wait_ge(c.q_taken, n(c.q_taken))
    rope_q(1)
    compressed(1)
    compressed_out(0)
    z()
    compressed_out(1)
    z()
    n.loop(pe, 2, lambda e, i: [chunk_products(e, n, c, group_slot(e, n, c), c.h_hi, c.h_lo, KT)
                                for _ in range(2)])
    half_norm_tensor(pe, n, c)
    for g in range(2):
        n.loop(pe, 2, lambda e, m: attend_tensor(e, n, c, nsa_units(c, g), c.pair_copied))
    half_norm_tensor(pe, n, c)
    pe.wait_ge(c.hid_lo_done, n(c.hid_lo_done, 8))
    n.loop(pe, 2, lambda e, i: [chunk_products(e, n, c, group_slot(e, n, c), c.hid_hi, c.hid_lo, KT)
                                for _ in range(2)])
    sum_squares(pe, n, c)


def half_norm_tensor(pe, n, c):
    for j in range(2):
        pe.wait_ge(c.half_sq, n(c.half_sq))
        for k in range(2):
            last = pe.matmul(c.m[1][:, :], c.ones[:, :], (c.sq, c.val)[j][:, k, :],
                             start=j == 0 and k == 0, stop=j == 1 and k == 1)
    last.then_inc(c.half_ssq, 1)


def half_norm_scalar(act, n, c, src):
    for j in range(2):
        act.activation((c.sq, c.val)[j][:, :, :], src[:, 2 * j:2 * j + 2, :], ACT.Square)\
            .then_inc(c.half_sq, 1)
    act.wait_ge(c.half_ssq, n(c.half_ssq))
    act.activation(c.gate[:, 0, 0:T], c.m[1][:, :], ACT.Sqrt, bias=c.eps, scale=1.0 / 512)\
        .then_inc(c.half_std, 1)


def half_norm_vector(dve, n, c, src):
    dve.wait_ge(c.half_std, n(c.half_std))
    dve.reciprocal(c.gate[:, 0, 0:T], c.gate[:, 0, 0:T]).then_inc(c.head_recip, 1)
    dve.wait_ge(c.head_recip, n(c.head_recip))
    for j in range(2):
        x = src[:, 2 * j:2 * j + 2, :]
        dve.tensor_tensor(x, x, over_tiles(c.gate[:, 0, 0:T]), ALU.mult).then_inc(c.half_done, 1)


def nsa_scalar(act, n, c, l, norm, post, a, out):
    act.wait_ge(c.nsa_free, n(c.nsa_free))
    act.dma_start(c.b_pos[:, :], a["pos"]).then_inc(c.pos_loaded, 16)
    act.dma_start(c.b_sel[:, :, :], a["b_sel"]).then_inc(c.sel_loaded, 16)
    act.dma_start(c.b_mask[:, :], a["b_mask"]).then_inc(c.b_masks_loaded, 16)
    act.dma_start(c.b_cmask[:, :, :], a["b_cmask"]).then_inc(c.b_masks_loaded, 16)
    act.dma_start(c.b_valid[:, :], a["b_valid"]).then_inc(c.b_masks_loaded, 16)
    act.dma_start(c.b_w2k[:, :, :], a["w2k"][l]).then_inc(c.w2_loaded, 16)
    act.dma_start(c.b_w2v[:, :, :], a["w2v"][l]).then_inc(c.w2_loaded, 16)
    split_next(act, n, c)
    norm_std(act, n, c)
    act.wait_ge(c.kc_taken, n(c.kc_taken))
    for par in range(2):
        for g in range(2):
            act.dma_start(c.b_r[64 * par:64 * par + 64, :, g, 0:T - par],
                          c.sq[64 * g:64 * g + 64, :, par:T]).then_inc(c.pairs_loaded, 16)
    split_next(act, n, c)
    for b in range(2):
        split_next(act, n, c)
        if b == 0:
            for t in (c.b_cos, c.b_sin):
                act.wait_ge(c.angle_ready, n(c.angle_ready))
                act.activation(t[:, :], t[:, :], ACT.Sin).then_inc(c.trig_ready, 1)
        act.wait_ge(c.tok_ready, n(c.tok_ready))
        act.activation(c.b_vs[:, b, :, :], c.m[3][:, :].rearrange("p (t f) -> p t f", t=TT), ACT.Copy)\
            .then_inc(c.tok_copied, 1)
    split_next(act, n, c)
    act.wait_ge(c.gates_turned, n(c.gates_turned))
    act.activation(c.b_g[:, :, :].rearrange("p t h -> p (t h)"), c.m[3][:, 0:TT * 24], ACT.Sigmoid)\
        .then_inc(c.gates_done, 1)
    split_next(act, n, c)
    for kv in range(2):
        split_next(act, n, c)
        act.wait_ge(c.a_ready, n(c.a_ready, 2))
        act.activation(c.b_a_hi[:, kv, 0:16 * BOTH], c.b_y[:, 2:4, :].rearrange("p t n -> p (t n)")
                       [:, 0:16 * BOTH], ACT.Copy).then_inc(c.a_hi_done, 1)
        split_next(act, n, c)
    for kv in range(2):
        act.wait_ge(c.cmp_taken, n(c.cmp_taken))
        act.activation(c.b_h[0:BOTH, :], c.b_h[0:BOTH, :], ACT.Gelu_apprx_tanh).then_inc(c.cmp_gelu, 1)
        act.wait_ge(c.cmp_turned, n(c.cmp_turned))
        act.activation(c.b_hT[:, :, 0:BOTH],
                       c.m[3][:, 0:P].rearrange("p (k n) -> p k n", k=2)[:, :, 0:BOTH], ACT.Copy)\
            .then_inc(c.cmp_hT, 1)
        act.wait_ge(c.cmp_out, n(c.cmp_out))
        if kv == 0:
            act.activation(c.b_kc[:, 0:BOTH], c.m[3][:, 0:BOTH], ACT.Copy).then_inc(c.cmp_copied, 1)
        else:
            act.activation(c.b_vc[0:N_CMP, :, :].rearrange("p g d -> p (g d)"),
                           c.m[3][0:N_CMP, 0:P], ACT.Copy).then_inc(c.cmp_copied, 1)
        split_next(act, n, c)
    n.loop(act, 2, lambda e, i: (split_next(e, n, c), split_next(e, n, c)))
    n.skip(c.group_taken, 14)
    act.wait_ge(c.conv_done, n(c.conv_done))
    half_norm_scalar(act, n, c, c.b_y)
    for g in range(2):
        n.loop(act, 2, lambda e, m: attend_scalar(e, n, c, nsa_units(c, g)))
    act.wait_ge(c.pair_taken, n(c.pair_taken, 4))
    half_norm_scalar(act, n, c, c.b_q)

    def hi(src, m, col):
        act.activation(c.hid_hi[:, m, :], src, ACT.Copy, scale=c.par[:, col:col + 1])\
            .then_inc(c.hid_hi_done, 1)
    act.wait_ge(c.half_done, n(c.half_done, 2))
    for m in range(4):
        hi(c.b_y[:, m, :], 4 + m, PC["con"] + 4 * l + m)
    act.wait_ge(c.half_done, n(c.half_done, 2))
    for m in range(4):
        hi(c.b_q[:, m, :], m, PC["aon"] + 4 * l + m)
    result_scalar(act, n, c, 1, norm, post)


def nsa_vector(dve, n, c, l, norm, post):
    rstd = over_tiles(c.rstd[:, :])

    def take(dst, part=P, mt=2):
        dve.wait_ge(c.chunk_done, n(c.chunk_done))
        dve.tensor_tensor(dst, c.ps[n.group % 2][0:part, 0:mt, :], over_tiles(c.rstd[0:part, :], mt),
                          ALU.mult).then_inc(c.group_taken, 1)
        n.group += 1
        dve.wait_ge(c.group_taken, n(c.group_taken))

    def signal(sem):
        dve.memset(c.stat[:, 8:9], 0.0).then_inc(sem, 1)

    def step(ins):
        ins.then_inc(c.nsa_step, 1)
        dve.wait_ge(c.nsa_step, n(c.nsa_step))

    norm_recip(dve, n, c)

    def rope_k(b):
        dst = (c.b_ks, c.b_kw)[b]
        signal(c.kv_taken)
        for g in range(2):
            dve.wait_ge(c.rope_ps, n(c.rope_ps))
            k = dst[:, g, :]
            dve.tensor_tensor(k, c.m[1][:, :], c.b_cos[:, :], ALU.mult)
            dve.tensor_tensor(c.b_ang[:, :], c.m[2][:, :], c.b_sin[:, :], ALU.mult)\
                .then_inc(c.rope_read, 1)
            dve.wait_ge(c.rope_read, n(c.rope_read))
            step(dve.tensor_tensor(k, k, c.b_ang[:, :], ALU.add))

    def rope_q(j):
        dve.wait_ge(c.rope_ps, n(c.rope_ps))
        q = c.b_qr[:, 2 * j:2 * j + 2, :]
        for k in range(2):
            last = dve.tensor_tensor(c.b_qr[:, 2 * j + k, :], c.m[1 + k][:, :], c.b_sin[:, :], ALU.mult)
        last.then_inc(c.rope_read, 1)
        for k in range(2):
            step(dve.tensor_tensor(c.b_ang[:, :], c.b_q[:, 2 * j + k, :], c.b_cos[:, :], ALU.mult))
            if k == 0:
                dve.wait_ge(c.rope_read, n(c.rope_read))
            step(dve.tensor_tensor(c.b_qr[:, 2 * j + k, :], c.b_qr[:, 2 * j + k, :], c.b_ang[:, :],
                                   ALU.add))

    def flat(kv):
        for g in range(2):
            o = c.b_y[:, 2:4, :].rearrange("p t n -> p (t n)")[:, 0:16 * BOTH]\
                .rearrange("p (j g n) -> p j g n", j=16, g=2)[:, :, g, :]
            src = c.b_r[:, kv, g, :].rearrange("p (n j t) -> p j n t", n=32, j=8)
            for half in range(2):
                x = src[:, :, half:half + N_CMP, 0]
                e = c.par[:, PC["pe"] + 32 * l + 16 * kv + 8 * half:][:, 0:8]
                last = dve.tensor_tensor(o[:, 8 * half:8 * half + 8, :], x,
                                         e.unsqueeze(2).to_broadcast([P, 8, N_CMP]), ALU.add)
            last.then_inc(c.a_ready, 1)
        dve.wait_ge(c.a_ready, n(c.a_ready, 2))
        dve.wait_ge(c.a_hi_done, n(c.a_hi_done))
        w = slice(0, 16 * BOTH)
        dve.tensor_tensor(c.b_a_lo[:, kv, w], c.b_y[:, 2:4, :].rearrange("p t n -> p (t n)")[:, w],
                          c.b_a_hi[:, kv, w].bitcast(F32), ALU.subtract).then_inc(c.a_lo_done, 1)

    take(c.sq[:, :, :])
    signal(c.kc_taken)
    dve.wait_ge(c.pos_loaded, n(c.pos_loaded, 16))
    step(dve.tensor_copy(c.b_ang[:, :], c.b_pos[:, :]))
    step(dve.tensor_scalar(c.b_ang[:, :], c.b_ang[:, :], c.par[:, PC["freq"]:PC["freq"] + 1], None,
                           ALU.mult))
    for t, quarter in ((c.b_cos, 0.25), (c.b_sin, 0.0)):
        turns = c.gate[:, 0, 0:T]
        step(dve.tensor_scalar(turns, c.b_ang[:, :], float(1 / (2 * np.pi)), quarter, ALU.mult, ALU.add))
        step(dve.tensor_scalar(turns, turns, ROUND, None, ALU.add))
        step(dve.tensor_scalar(turns, turns, ROUND, None, ALU.subtract))
        step(dve.scalar_tensor_tensor(t[:, :], turns, -TWO_PI[0], c.b_ang[:, :], ALU.mult, ALU.add))
        step(dve.scalar_tensor_tensor(t[:, :], turns, -TWO_PI[1], t[:, :], ALU.mult, ALU.add))
        step(dve.scalar_tensor_tensor(t[:, :], turns, -TWO_PI[2], t[:, :], ALU.mult, ALU.add))
        step(dve.tensor_scalar(t[:, :], t[:, :], float(2 * np.pi * quarter), 3.1415925, ALU.add, ALU.min))
        dve.tensor_scalar(t[:, :], t[:, :], -3.1415925, None, ALU.max).then_inc(c.angle_ready, 1)
    take(c.val[:, :, :])
    dve.wait_ge(c.trig_ready, n(c.trig_ready, 2))
    rope_k(0)
    take(c.b_y[:, 0:2, :])
    rope_k(1)
    dve.wait_ge(c.chunk_done, n(c.chunk_done))
    dve.tensor_tensor(c.acc[0:24, 0, :], c.ps[n.group % 2][0:24, 0, :], c.rstd[0:24, :], ALU.mult)\
        .then_inc(c.group_taken, 1)
    n.group += 1
    dve.wait_ge(c.group_taken, n(c.group_taken))
    signal(c.gates_taken)
    dve.wait_ge(c.pairs_loaded, n(c.pairs_loaded, 64))
    take(c.b_q[:, 0:2, :])
    signal(c.q_taken)
    flat(0)
    rope_q(0)
    take(c.b_q[:, 2:4, :])
    signal(c.q_taken)
    flat(1)
    rope_q(1)
    for kv in range(2):
        n.skip(c.chunk_done)
        dve.wait_ge(c.chunk_done, n(c.chunk_done))
        if kv == 1:
            dve.wait_ge(c.cmp_hT, n(c.cmp_hT))
        dve.tensor_copy(c.b_h[0:BOTH, :], c.ps[n.group % 2][0:BOTH, 0, 0:CW]).then_inc(c.group_taken, 1)
        n.group += 1
        dve.wait_ge(c.group_taken, n(c.group_taken))
        signal(c.cmp_taken)
    n.skip(c.cmp_hT)
    for j in range(2):
        take(c.b_u[:, 2 * j:2 * j + 2, :])
    for j in range(2):
        take(c.val[:, :, :])
        u = c.b_u[:, 2 * j:2 * j + 2, :]
        step(dve.tensor_tensor(u, u, c.val[:, :, :], ALU.mult))
        for m in (2 * j, 2 * j + 1):
            w = [c.par[:, PC["cw"] + 12 * l + 4 * k + m:][:, 0:1] for k in range(3)]
            step(dve.tensor_scalar(c.b_y[:, m, :], c.b_u[:, m, :], w[2], None, ALU.mult))
            for k, s in ((1, 1), (0, 2)):
                step(dve.scalar_tensor_tensor(c.b_y[:, m, s:], c.b_u[:, m, 0:T - s], w[k],
                                              c.b_y[:, m, s:], ALU.mult, ALU.add))
    for j in range(2):
        take(c.val[:, :, :])
        y = c.b_y[:, 2 * j:2 * j + 2, :]
        step(dve.tensor_tensor(y, y, c.val[:, :, :], ALU.mult))
    signal(c.conv_done)
    half_norm_vector(dve, n, c, c.b_y)
    dve.wait_ge(c.b_masks_loaded, n(c.b_masks_loaded, 48))
    dve.wait_ge(c.w2_loaded, n(c.w2_loaded, 32))
    dve.wait_ge(c.gates_done, n(c.gates_done))
    dve.wait_ge(c.cmp_copied, n(c.cmp_copied, 2))

    def pair(e, m, g):
        m = 2 * g + m
        e.tensor_copy(c.qs[:, :], tile(c.b_q, m))
        e.tensor_copy(c.qs2[:, :], tile(c.b_qr, m))
        e.tensor_copy(c.gp[:, :].rearrange("p (t h) -> p t h", t=TT), c.b_g[:, :, bass.ds(6 * m, 6)])\
            .then_inc(c.gp_copied, 1)
        e.wait_ge(c.gp_copied, n(c.gp_copied))
        for hh in range(2):
            last = e.tensor_tensor(c.gp[:, 3 * hh:3 * hh + 1], c.gp[:, 3 * hh:3 * hh + 1],
                                   c.b_valid[:, 0:1], ALU.mult)
        last.then_inc(c.pair_copied, 1)
        attend_vector(e, n, c, nsa_units(c, g), NSA_SCALE)
        e.wait_ge(c.pair_ready, n(c.pair_ready))
        carry(e, c)
        e.tensor_copy(tile(c.b_q, m), c.m[3][:, :]).then_inc(c.pair_taken, 1)
    for g in range(2):
        n.loop(dve, 2, lambda e, m: pair(e, m, g))
    dve.wait_ge(c.pair_taken, n(c.pair_taken, 4))
    half_norm_vector(dve, n, c, c.b_q)

    def low(src, m, col):
        dve.wait_ge(c.hid_hi_done, n(c.hid_hi_done))
        dve.scalar_tensor_tensor(c.hid_lo[:, m, :], src, c.par[:, col:col + 1],
                                 c.hid_hi[:, m, :].bitcast(F32), ALU.mult, ALU.subtract)\
            .then_inc(c.hid_lo_done, 1)
    n.skip(c.half_done, 2)
    dve.wait_ge(c.half_done, n(c.half_done, 2))
    for m in range(4):
        low(c.b_y[:, m, :], 4 + m, PC["con"] + 4 * l + m)
    step(dve.memset(c.stat[:, 8:9], 0.0))
    for m in range(4):
        low(c.b_q[:, m, :], m, PC["aon"] + 4 * l + m)
    result_vector(dve, n, c, 1, norm, post)


def build(nc, a, out, plan, n_chunks):
    ctx = ExitStack()
    with ctx:
        c = Core(nc, ctx)
        block = ctx.enter_context(nc.Block())

        def each_pair(eng, n, first, body):
            for s in range(2):
                body(eng, s, s, True)
            pairs = n_chunks // 2
            n.loop(eng, pairs - 1, lambda e, i: [body(e, 2 * i + 2 + s, s, False) for s in range(2)])
            if n_chunks % 2:
                body(eng, n_chunks - 1, 0, False)

        @block.sync
        def _(sp):
            n = Count()
            sp.dma_start(c.par[:, :], a["par"]).then_inc(c.params_loaded, 16)
            sp.dma_start(c.x[:, :, :], a["xT"]).then_inc(c.x_loaded, 16)

            def load(e, chunk, s, first):
                if not first:
                    e.wait_ge(c.w_lo_done, n(c.w_lo_done))
                e.dma_start(c.stage[:, s, :], a["w"][bass.ds(chunk, 1), :, :]
                            .rearrange("o p n -> (o p) n")).then_inc(c.w_loaded[s], 16)
            each_pair(sp, n, True, load)

        @block.gpsimd
        def _(pool):
            n = Count()

            def low_part(e, chunk, s, first):
                e.wait_ge(c.w_hi_done, n(c.w_hi_done))
                hi = c.w_hi[:, s, :, :].rearrange("p k n -> p (k n)")
                e.tensor_tensor(c.w_lo[:, s, :, :].rearrange("p k n -> p (k n)"), c.stage[:, s, :],
                                hi.bitcast(F32), ALU.subtract).then_inc(c.w_lo_done, 1)
            each_pair(pool, n, True, low_part)

        @block.tensor
        def _(pe):
            n = Count()
            for kind, kw in plan:
                TENSOR[kind](pe, n, c, **kw)

        @block.scalar
        def _(act):
            n = Count()
            act.dma_start(c.ident[:, :], a["ident"]).then_inc(c.ident_loaded, 16)
            act.dma_start(c.blockones[:, :], a["blockones"]).then_inc(c.blockones_loaded, 16)
            act.dma_start(c.ones[:, :], a["ones"]).then_inc(c.ones_loaded, 16)
            act.wait_ge(c.params_loaded, 16)
            act.wait_ge(c.x_loaded, 16)
            act.wait_ge(c.eps_ready, 1)
            split_next(act, n, c)
            for kind, kw in plan:
                SCALAR[kind](act, n, c, a=a, out=out, **kw)

        @block.vector
        def _(dve):
            n = Count()
            dve.wait_ge(c.params_loaded, 16)
            dve.wait_ge(c.x_loaded, 16)
            for l in range(2):
                for f in (0, 2):
                    at = PC["post"] + 8 * (3 * l + f)
                    dve.tensor_scalar(c.par[:, at:at + 8], c.par[:, at:at + 8], 0.5, None, ALU.mult)
            dve.memset(c.eps, EPS).then_inc(c.eps_ready, 1)
            for kind, kw in plan:
                VECTOR[kind](dve, n, c, **kw)


def first_scalar(act, n, c, norm, a, out):
    n.loop(act, 4, lambda e, m: next_h_scalar(e, n, c, m, None, norm))


def first_vector(dve, n, c, norm):
    clear_squares(dve, n, c)
    n.loop(dve, 4, lambda e, m: next_h_vector(e, n, c, m, norm))
    n.skip(c.acc_ready)


def ffn_tensor(pe, n, c, conv, norm, post):
    if n.group == 0:
        pe.wait_ge(c.ones_loaded, 16)
    ffn_in_tensor(pe, n, c)
    ffn_down_tensor(pe, n, c)
    if post is not None:
        sum_squares(pe, n, c)


def ffn_scalar(act, n, c, conv, norm, post, a, out):
    ffn_in_scalar(act, n, c, conv)
    result_scalar(act, n, c, 3, norm, post)


def ffn_vector(dve, n, c, conv, norm, post):
    ffn_in_vector(dve, n, c, conv)
    result_vector(dve, n, c, 3, norm, post)


def last_scalar(act, n, c, a, out):
    act.wait_ge(c.last_ready, 1)
    act.dma_start(out, c.x[:, :, :]).then_inc(c.stored, 16)
    act.wait_ge(c.stored, 16)


def last_vector(dve, n, c):
    dve.wait_ge(c.x_ready, n(c.x_ready, 0))
    dve.memset(c.stat[:, 10:11], 0.0).then_inc(c.last_ready, 1)


def free_vector(dve, n, c):
    dve.memset(c.stat[:, 10:11], 0.0).then_inc(c.nsa_free, 1)


def nothing(*_, **__):
    pass


TENSOR = {"nsa": nsa_tensor, "odd": odd_tensor, "even": even_tensor, "first": nothing, "free": nothing, "ffn": ffn_tensor, "last": nothing}
SCALAR = {"free": nothing, "nsa": nsa_scalar, "odd": odd_scalar, "even": even_scalar, "first": first_scalar, "ffn": ffn_scalar, "last": last_scalar}
VECTOR = {"free": free_vector, "nsa": nsa_vector, "odd": odd_vector, "even": even_vector, "first": first_vector, "ffn": ffn_vector, "last": last_vector}


def plan_phases():
    plan = [("first", dict(norm=0)), ("even", dict(norm=1)), ("ffn", dict(conv=0, norm=2, post=None)),
            ("odd", dict(norm=3)), ("ffn", dict(conv=1, norm=4, post=None))]
    for l in range(2):
        after = 4 + 3 * (l + 1) if l == 0 else None
        plan += [("ffn", dict(conv=None, norm=5 + 3 * l, post=3 * l)), ("free", {}),
                 ("nsa", dict(l=l, norm=6 + 3 * l, post=3 * l + 1)),
                 ("ffn", dict(conv=None, norm=after, post=3 * l + 2))]
    return plan + [("last", {})]


def weight_chunks(w):
    rows, cols = w.shape
    out = np.zeros((cols // CW, P, KT, CW), np.float32)
    k = rows // P
    out[:, :, :k] = w.reshape(k, P, cols // CW, CW).transpose(2, 1, 0, 3)
    return out.reshape(-1, P, CHUNK)


def padded(w):
    return np.concatenate([w, np.zeros((w.shape[0], CW - w.shape[1]), np.float32)], axis=1)


def ffn_chunks(gate, up, down):
    g, u = weight_chunks(gate), weight_chunks(up)
    both = np.stack([g, u], axis=1).reshape(-1, P, CHUNK)
    parts = [weight_chunks(down[D * j:min(D * (j + 1), FF)]) for j in range(3)]
    return [both, np.stack(parts, axis=1).reshape(-1, P, CHUNK)]


def all_chunks(a):
    w = a["ev_w_in"][0]
    out = [weight_chunks(np.concatenate([w[:, 1024:], w[:, 512:1024], w[:, :512]], axis=1)),
           weight_chunks(a["ev_w_out"][0])]
    out += ffn_chunks(a["ffn_w_gate"][0], a["ffn_w_up"][0], a["ffn_w_down"][0])
    w = a["od_w_in"][0]
    out += [weight_chunks(padded(w[:, 3072:])), weight_chunks(w[:, :3072]),
            weight_chunks(a["od_w_out"][0])]
    out += ffn_chunks(a["ffn_w_gate"][1], a["ffn_w_up"][1], a["ffn_w_down"][1])
    for l in range(2):
        out += ffn_chunks(*(a[f"ffn1_w_{x}_2"][l] for x in ("gate", "up", "down")))
        w = a["w_in_2"][l]
        out += [weight_chunks(w[:, 512:1280]), weight_chunks(padded(w[:, 1280:1304])),
                weight_chunks(w[:, :512])]
        for x in "kv":
            out += [weight_chunks(a[f"cmp_w1_{x}_2"][l][D * h:D * (h + 1)]) for h in range(2)]
        out += [weight_chunks(w[:, 1816:]), weight_chunks(w[:, 1304:1816]),
                weight_chunks(a["w_out_2"][l])]
        out += ffn_chunks(*(a[f"ffn2_w_{x}_2"][l] for x in ("gate", "up", "down")))
    return np.concatenate(out + [np.zeros((1, P, CHUNK), np.float32)])


def parameters(a):
    par = np.zeros((P, PCOLS), np.float32)

    def put(name, off, v):
        v = v.reshape(-1, P).T
        par[:, PC[name] + off:PC[name] + off + v.shape[1]] = v

    norms = [a["norm_mix_g"][0], a["norm_ffn_g"][0], a["norm_mix_g"][1], a["norm_ffn_g"][1]]
    for l in range(2):
        norms += [a["ffn1_norm_pre_2"][l], a["mix_norm_pre_2"][l], a["ffn2_norm_pre_2"][l]]
        for i, x in enumerate(("ffn1", "mix", "ffn2")):
            put("post", 8 * (3 * l + i), a[f"{x}_norm_post_2"][l])
        put("pe", 32 * l, a["cmp_pe_k_2"][l])
        put("pe", 32 * l + 16, a["cmp_pe_v_2"][l])
    for i, g in enumerate(norms):
        put("norm", 8 * i, g)
    for name, x in (("lng", "ev_a_ln_g"), ("lnb", "ev_a_ln_b"), ("fcw", "ffn_conv_w"),
                    ("fcb", "ffn_conv_b"), ("ba", "od_b_a"), ("hg", "od_head_g"),
                    ("cw", "conv_w_2"), ("aon", "attn_out_norm_2"), ("con", "conv_out_norm_2")):
        put(name, 0, a[x])
    put("qkg", 0, np.tile(a["ev_q_g"][0], 2))
    put("qkg", 1, np.tile(a["ev_k_g"][0], 2))
    d = np.arange(P) % HD
    freq = np.float32(500000.0) ** (-(d % 8).astype(np.float32) * np.float32(2.0 / 16))
    par[:, PC["freq"]] = np.where(d < 16, freq, 0)
    return par


def constants():
    p = np.arange(P)
    q, k = p[:, None], p[None, :]
    dist = q - np.arange(T)[None, :] + 384
    times = sum(((dist >= 0) & (dist <= window) & (dist % step == 0)).astype(int)
                for window, step in ((128, 1), (512, 4), (2048, 16)))
    ev_mask = np.where(times > 0, np.log(np.maximum(times, 1)) / EVEN_SCALE, NEG)
    reset = np.ones((P, T), np.float32)
    reset[:, ::C_CHUNK] = 0
    cmask = np.full((P, TT, 32), NEG, np.float32)
    block = np.arange(N_CMP)
    for i in range(TT):
        cmask[:, i, :N_CMP] = np.where(16 * block[None, :] + 31 <= P * i + q, 0, NEG)
    turn = np.zeros((P, P), np.float32)
    double = np.zeros((2, P, P), np.float32)
    turned = np.zeros((2, P, P), np.float32)
    for h in (0, HD):
        for d in range(8):
            turn[h + d + 8, h + d] = -1
            turn[h + d, h + d + 8] = 1
            for g in range(2):
                turned[g, g * HD + d + 8, h + d] = -1
                turned[g, g * HD + d, h + d + 8] = 1
        for d in range(HD):
            for g in range(2):
                double[g, g * HD + d, h + d] = 1
    return dict(
        ident=np.eye(P, dtype=np.float32), ones=np.ones((P, P), np.float32),
        blockones=(q // HD == k // HD).astype(np.float32), tri=(q <= k).astype(np.float32),
        ev_mask=ev_mask.astype(np.float32), od_reset=reset,
        od_mask=((q // C_CHUNK == k // C_CHUNK) & (q <= k)).astype(np.int32),
        b_mask=np.where(dist >= 0, 0, NEG).astype(np.float32), b_cmask=cmask,
        b_valid=(q >= 31).astype(np.float32),
        b_sel=np.ascontiguousarray(np.stack([double[0], turned[0], double[1], turned[1], turn], axis=1)))


def kernel(**inputs):
    import concourse.bacc as _bacc
    from concourse import mybir as _mybir
    from concourse.bass_utils import run_bass_kernel_spmd as _run

    a = {k: np.asarray(v) for k, v in inputs.items()}
    arrays = constants()
    arrays["par"] = parameters(a)
    arrays["w"] = all_chunks(a)
    arrays["xT"] = np.ascontiguousarray(a["x"][0].T.reshape(KT, P, T).transpose(1, 0, 2))
    arrays["pos"] = np.ascontiguousarray(np.broadcast_to(a["positions_2"], (P, T)))
    arrays["ev_ws"] = np.ascontiguousarray(a["ev_a_ws"][0].transpose(2, 0, 1))
    arrays["ev_bs"] = np.ascontiguousarray(
        np.repeat(a["ev_a_bs"][0].reshape(4, 2, P), HD, axis=1).transpose(1, 0, 2))
    arrays["od_wa"] = np.ascontiguousarray(a["od_w_a2"][0])
    for x in "kv":
        w2 = a[f"cmp_w2_{x}_2"].reshape(2, 2, P, HD).transpose(0, 2, 1, 3)
        arrays[f"w2{x}"] = np.ascontiguousarray(np.concatenate([w2, w2], axis=3) if x == "k" else w2)

    nc = _bacc.Bacc("TRN2", target_bir_lowering=False, num_devices=1)
    args = {k: nc.dram_tensor(f"in_{k}", v.shape, _mybir.dt.from_np(v.dtype), kind="ExternalInput").ap()
            for k, v in arrays.items()}
    out = nc.dram_tensor("out_x", [P, KT, T], _mybir.dt.float32, kind="ExternalOutput").ap()
    build(nc, args, out, plan_phases(), arrays["w"].shape[0])
    r = _run(nc, [{f"in_{k}": v for k, v in arrays.items()}], core_ids=[0])
    y = np.asarray(r.results[0]["out_x"])
    return np.ascontiguousarray(y.transpose(2, 1, 0).reshape(1, T, D))
```
